# Optimizing a Trainium2 kernel written in Bass

```python
import jax, jax.numpy as jnp
from jax import lax
import numpy as np

D_MODEL = 1024
BATCH = 1
SEQ = 512
DEPTH = 1

SGU_WIDTH = D_MODEL
SGU_GROUPS = 8
SGU_GROUP_DIM = SGU_WIDTH // SGU_GROUPS
CHUNK = 128
HEAD_DIM = 64
N_Q_HEADS = D_MODEL // HEAD_DIM
N_KV_HEADS = N_Q_HEADS // 4
Q_PER_KV = N_Q_HEADS // N_KV_HEADS
WINDOW = 128
BLOCK = 128
ROPE_DIM = HEAD_DIM // 4
ROPE_THETA = 500000.0
ATTN_WIDTH = N_Q_HEADS * HEAD_DIM
KV_WIDTH = N_KV_HEADS * HEAD_DIM
D_FF = 4 * D_MODEL
EPS = 1e-6

IN_SPLITS = (SGU_WIDTH, SGU_WIDTH, ATTN_WIDTH, KV_WIDTH, KV_WIDTH, D_MODEL, D_MODEL)
IN_WIDTH = sum(IN_SPLITS)

kernel_name = "hybrid_gated_sgu_swa_sink_block"

def rms_norm(x, g):
    xf = x.astype(jnp.float32)
    y = xf * lax.rsqrt(jnp.mean(xf * xf, axis=-1, keepdims=True) + EPS)
    return (y * g.astype(jnp.float32)).astype(x.dtype)

def layer_norm(x, g, b):
    xf = x.astype(jnp.float32)
    mu = jnp.mean(xf, axis=-1, keepdims=True)
    var = jnp.mean(jnp.square(xf - mu), axis=-1, keepdims=True)
    y = (xf - mu) * lax.rsqrt(var + EPS)
    return (y * g.astype(jnp.float32) + b.astype(jnp.float32)).astype(x.dtype)

def partial_rotary(x, positions):
    inv_freq = ROPE_THETA ** (-jnp.arange(0, ROPE_DIM, 2, dtype=jnp.float32) / ROPE_DIM)
    ang = positions.astype(jnp.float32)[..., None] * inv_freq
    cos = jnp.cos(ang)[:, :, None, :]
    sin = jnp.sin(ang)[:, :, None, :]
    xr = x[..., :ROPE_DIM].astype(jnp.float32)
    x1, x2 = xr[..., : ROPE_DIM // 2], xr[..., ROPE_DIM // 2:]
    rot = jnp.concatenate([x1 * cos - x2 * sin, x2 * cos + x1 * sin], axis=-1).astype(x.dtype)
    return jnp.concatenate([rot, x[..., ROPE_DIM:]], axis=-1)

def chunked_spatial_gating(u, v, ln_g, ln_b, w_s, b_s):
    B, S, _ = v.shape
    n_chunks = S // CHUNK
    vn = layer_norm(v, ln_g, ln_b)
    vc = vn.reshape(B, n_chunks, CHUNK, SGU_GROUPS, SGU_GROUP_DIM)
    causal = jnp.tril(jnp.ones((CHUNK, CHUNK), dtype=bool))
    w = jnp.where(causal[None], w_s, jnp.zeros_like(w_s))
    mixed = jnp.einsum('gts,bcsge->bctge', w, vc) + b_s.T[None, None, :, :, None]
    return u * mixed.reshape(B, S, SGU_WIDTH)

def sliding_window_sink_attention(q, k, v, sinks):
    B, S = q.shape[0], q.shape[1]
    n_blocks = S // BLOCK
    qb = q.reshape(B, n_blocks, BLOCK, N_KV_HEADS, Q_PER_KV, HEAD_DIM)
    kb = k.reshape(B, n_blocks, BLOCK, N_KV_HEADS, HEAD_DIM)
    vb = v.reshape(B, n_blocks, BLOCK, N_KV_HEADS, HEAD_DIM)
    pad = ((0, 0), (1, 0), (0, 0), (0, 0), (0, 0))
    k_band = jnp.concatenate([jnp.pad(kb, pad)[:, :-1], kb], axis=2)
    v_band = jnp.concatenate([jnp.pad(vb, pad)[:, :-1], vb], axis=2)
    scores = jnp.einsum('bnqgrd,bnkgd->bngrqk', qb, k_band).astype(jnp.float32) * (HEAD_DIM ** -0.5)
    blk = jnp.arange(n_blocks)[:, None]
    qpos = blk * BLOCK + jnp.arange(BLOCK)[None, :]
    kpos = (blk - 1) * BLOCK + jnp.arange(2 * BLOCK)[None, :]
    diff = qpos[:, :, None] - kpos[:, None, :]
    allowed = (diff >= 0) & (diff < WINDOW) & (kpos[:, None, :] >= 0)
    scores = jnp.where(allowed[None, :, None, None], scores, jnp.float32(-1e30))
    sink = sinks.astype(jnp.float32).reshape(N_KV_HEADS, Q_PER_KV)[None, None, :, :, None, None]
    m = jnp.maximum(jnp.max(scores, axis=-1, keepdims=True), sink)
    p = jnp.exp(scores - m)
    denom = jnp.sum(p, axis=-1, keepdims=True) + jnp.exp(sink - m)
    p = (p / denom).astype(v.dtype)
    out = jnp.einsum('bngrqk,bnkgd->bnqgrd', p, v_band)
    return out.reshape(B, S, ATTN_WIDTH)

def hybrid_layer(x, positions, w_in, ln_v_gain, ln_v_bias, w_spatial, b_spatial, sinks,
                 w_a, w_b, w_o, norm_mix_pre, norm_mix_post,
                 w_ff_in, w_ff_out, norm_ff_pre, norm_ff_post):
    B, S, _ = x.shape
    h = rms_norm(x, norm_mix_pre)
    proj = h @ w_in
    offs = np.cumsum(IN_SPLITS)[:-1].tolist()
    u, v_sgu, q, k, v_att, gate_a, gate_b = jnp.split(proj, offs, axis=-1)
    a = chunked_spatial_gating(jax.nn.gelu(u), jax.nn.gelu(v_sgu), ln_v_gain, ln_v_bias, w_spatial, b_spatial)
    q = partial_rotary(q.reshape(B, S, N_Q_HEADS, HEAD_DIM), positions)
    k = partial_rotary(k.reshape(B, S, N_KV_HEADS, HEAD_DIM), positions)
    v_att = v_att.reshape(B, S, N_KV_HEADS, HEAD_DIM)
    att = sliding_window_sink_attention(q, k, v_att, sinks)
    merged = jax.nn.sigmoid(gate_a) * (a @ w_a) + jax.nn.sigmoid(gate_b) * (att @ w_b)
    x = x + rms_norm(merged @ w_o, norm_mix_post)
    hf = rms_norm(x, norm_ff_pre)
    ff = jnp.square(jax.nn.relu(hf @ w_ff_in)) @ w_ff_out
    return x + rms_norm(ff, norm_ff_post)

def setup_inputs(seed: int = 0) -> dict:
    key = jax.random.key(seed)
    ks = jax.random.split(key, 20)
    f32 = jnp.float32
    def nrm(k, shape, scale):
        return jax.random.normal(k, shape, dtype=f32) * scale
    def gain(k, shape):
        return 1.0 + 0.05 * jax.random.normal(k, shape, dtype=f32)
    x = jax.random.normal(ks[0], (BATCH, SEQ, D_MODEL), dtype=f32)
    offset = jax.random.randint(ks[1], (BATCH, 1), 0, 4096, dtype=jnp.int32)
    positions = offset + jnp.arange(SEQ, dtype=jnp.int32)[None, :]
    return {
        "x": x,
        "positions": positions,
        "w_in": nrm(ks[2], (DEPTH, D_MODEL, IN_WIDTH), D_MODEL ** -0.5),
        "ln_v_gain": gain(ks[3], (DEPTH, SGU_WIDTH)),
        "ln_v_bias": nrm(ks[4], (DEPTH, SGU_WIDTH), 0.02),
        "w_spatial": nrm(ks[5], (DEPTH, SGU_GROUPS, CHUNK, CHUNK), CHUNK ** -0.5),
        "b_spatial": gain(ks[6], (DEPTH, SGU_GROUPS, CHUNK)),
        "sinks": nrm(ks[7], (DEPTH, N_Q_HEADS), 0.5),
        "w_a": nrm(ks[8], (DEPTH, SGU_WIDTH, D_MODEL), SGU_WIDTH ** -0.5),
        "w_b": nrm(ks[9], (DEPTH, ATTN_WIDTH, D_MODEL), ATTN_WIDTH ** -0.5),
        "w_o": nrm(ks[10], (DEPTH, D_MODEL, D_MODEL), D_MODEL ** -0.5),
        "norm_mix_pre": gain(ks[11], (DEPTH, D_MODEL)),
        "norm_mix_post": gain(ks[12], (DEPTH, D_MODEL)),
        "w_ff_in": nrm(ks[13], (DEPTH, D_MODEL, D_FF), D_MODEL ** -0.5),
        "w_ff_out": nrm(ks[14], (DEPTH, D_FF, D_MODEL), D_FF ** -0.5),
        "norm_ff_pre": gain(ks[15], (DEPTH, D_MODEL)),
        "norm_ff_post": gain(ks[16], (DEPTH, D_MODEL)),
    }

def reference(x, positions, w_in, ln_v_gain, ln_v_bias, w_spatial, b_spatial, sinks,
              w_a, w_b, w_o, norm_mix_pre, norm_mix_post,
              w_ff_in, w_ff_out, norm_ff_pre, norm_ff_post):
    for l in range(DEPTH):
        x = hybrid_layer(x, positions, w_in[l], ln_v_gain[l], ln_v_bias[l], w_spatial[l], b_spatial[l],
                         sinks[l], w_a[l], w_b[l], w_o[l], norm_mix_pre[l], norm_mix_post[l],
                         w_ff_in[l], w_ff_out[l], norm_ff_pre[l], norm_ff_post[l])
    return x


_drawn_inputs = setup_inputs


def setup_inputs(seed=0):
    import zlib

    import numpy as np

    out = dict(_drawn_inputs(seed))
    spreads = {}
    factors = {'ln_v_gain': 2.96, 'ln_v_bias': 7.304, 'sinks': 8.0}
    for name, (base, spread) in spreads.items():
        noise = np.random.default_rng([zlib.crc32(name.encode()), seed]).standard_normal(out[name].shape)
        drawn = base * np.exp(spread * noise) if base else spread * noise
        out[name] = __import__('jax').numpy.asarray(drawn.astype(out[name].dtype))
    for name, factor in factors.items():
        out[name] = (out[name] * factor).astype(out[name].dtype)
    return out
```

```python
from contextlib import ExitStack

import numpy as np

import concourse.bass as bass
from concourse import mybir

F32 = mybir.dt.float32
F32R = mybir.dt.float32r
I32 = mybir.dt.int32
ACT = mybir.ActivationFunctionType
ALU = mybir.AluOpType

P = 128
D = 1024
S = 512
TT = S // P
KT = D // P
HD = 64
NQ = D // HD
NKV = NQ // 4
QPK = NQ // NKV
NH = NQ + 2 * NKV
ROT = HD // 4 // 2
GROUPS = 8
FF = 4 * D
IN_W = 3 * D + 2 * NKV * HD + 2 * D
EPS = 1e-6
NEG = -1e30
SLOTS = 4
UNIT = KT * P
COL = 512

C_U, C_V, C_Q = 0, D, 2 * D
C_KV = C_Q + D
C_GATES = C_KV + 2 * NKV * HD

U_QKV = 0
U_GATE = U_QKV + 12
U_WB = U_GATE + 16
U_VSGU = U_WB + 8
U_U = U_VSGU + 8
U_WA = U_U + 8
U_WO = U_WA + 8
U_FF = U_WO + 8
HALF_K = FF // P // 2
U_HALF = 2 * HALF_K
UNITS = U_FF + 2 * U_HALF

def _pe_counts():
    unit_done, bank_done, n = {}, {}, 0

    def columns(first, units):
        nonlocal n
        for u in range(first, first + units):
            n += 1
            unit_done[u] = bank_done[u, 0] = n

    def rows(first, units, inside=SLOTS):
        nonlocal n
        last = first + units - 1
        for u in range(first, min(first + inside, last)):
            n += 1
            unit_done[u] = n
        if inside < units:
            for t in range(TT - 1):
                n += 1
                bank_done[last, t] = n
            for u in range(first + inside, last + 1):
                n += 1
                unit_done[u] = n
            bank_done[last, TT - 1] = n
        else:
            for t in range(TT):
                n += 1
                bank_done[last, t] = n
            unit_done[last] = n

    for b in range(3):
        rows(U_QKV + b * SLOTS, SLOTS)
    columns(U_GATE, 16)
    columns(U_WB, KT)
    rows(U_VSGU, SLOTS)
    rows(U_VSGU + SLOTS, SLOTS)
    columns(U_U, KT)
    columns(U_WA, KT)
    rows(U_WO, SLOTS)
    rows(U_WO + SLOTS, SLOTS, inside=0)
    for c in range(2):
        first = U_FF + c * U_HALF
        columns(first, HALF_K)
        rows(first + HALF_K, HALF_K // 2, inside=HALF_K // 2)
        rows(first + HALF_K + HALF_K // 2, HALF_K // 2, inside=SLOTS if c else HALF_K // 2)
    return unit_done, bank_done


UNIT_DONE, BANK_DONE = _pe_counts()
BLOCK_COUNTS = SLOTS - 1 + TT

GATES_AHEAD = 4
STEPS = TT * NKV
LAG = 2
SLOT_COUNT = STEPS + LAG
GATE_K_STEPS = (16 - GATES_AHEAD) * KT


NORM_ORDER = [(2, 0), (2, 1), (3, 0), (2, 2), (3, 1), (2, 3), (3, 2), (3, 3)]


def k_steps_until(slot):
    return -(-GATE_K_STEPS * (slot + 1) // SLOT_COUNT)


def gates_finished(slot):
    before = k_steps_until(slot - 1) // KT if slot else 0
    return range(GATES_AHEAD + before, GATES_AHEAD + k_steps_until(slot) // KT)


def mix_groups_after(unit):
    return {2: [0], 3: [1, 2], 4: [3, 4], 5: [5], 6: [6], 7: [7]}.get(unit, [])


def _two_pi_parts():
    rest, parts = 2 * np.pi, []
    for low in (-9, -21, -33):
        part = np.floor(rest * 2.0 ** -low) * 2.0 ** low
        parts.append(float(part))
        rest -= part
    return parts + [float(np.float32(rest))]


TWO_PI = _two_pi_parts()
ROUND = 1.5 * 2.0 ** 23
PI32 = 3.1415925
INV_FREQ = [float(np.float32(500000.0 ** (-2 * i / (2 * ROT)))) for i in range(ROT)]


def hybrid_block(nc, x, positions, w_in, ln_v_gain, ln_v_bias, w_spatial, b_spatial, sinks, w_a, w_b,
                 w_o, norm_mix_pre, norm_mix_post, w_ff_in, w_ff_out, norm_ff_pre, norm_ff_post, out):
    x_v = x[0].rearrange("(t p) d -> p t d", p=P)
    out_v = out[0].rearrange("(t p) d -> p t d", p=P)
    pos_v = positions[0].rearrange("(t p) -> p t", p=P)

    def rows(w):
        return w[0].rearrange("(k p) n -> p k n", p=P)

    w_in_v, w_a_v, w_b_v, w_o_v = rows(w_in), rows(w_a), rows(w_b), rows(w_o)
    w_ff_in_v, w_ff_out_v = rows(w_ff_in), rows(w_ff_out)

    with ExitStack() as ctx:
        def sem(name):
            return ctx.enter_context(nc.semaphore(name))

        def keep(name, shape, dt=F32):
            return ctx.enter_context(nc.sbuf_tensor(name, shape, dt))

        w_raw = keep("w_raw", [P, SLOTS, UNIT])
        w_hi = keep("w_hi", [P, SLOTS, UNIT], F32R)
        w_lo = keep("w_lo", [P, SLOTS, UNIT], F32R)
        actB_hi = keep("actB_hi", [P, KT, S], F32R)
        actB_lo = keep("actB_lo", [P, KT, S], F32R)
        w_mix = keep("w_mix", [P, GROUPS, P])
        ident = keep("ident", [P, P])
        mask = keep("mask", [P, 2 * P])
        g_mix_post = keep("g_mix_post", [P, D])
        g_pre = keep("g_pre", [P, KT])
        g_ff_pre = keep("g_ff_pre", [P, KT])
        pos_i = keep("pos_i", [P, TT], I32)
        pos_f = keep("pos_f", [P, TT])
        inv_freq = keep("inv_freq", [P, ROT])
        ang = keep("ang", [P, TT, ROT])
        turns = keep("turns", [P, TT, ROT])
        turns_hi = keep("turns_hi", [P, TT, ROT])
        sin_arg = keep("sin_arg", [P, TT, ROT])
        cos_arg = keep("cos_arg", [P, TT, ROT])
        sin_t = keep("sin_t", [P, TT, ROT])
        cos_t = keep("cos_t", [P, TT, ROT])
        sink_b = keep("sink_b", [P, NQ])
        neg_sink = keep("neg_sink", [P, NQ])
        ssq = keep("ssq", [P, 4, TT])
        ssq2 = keep("ssq2", [P, TT])
        var_eps = keep("var_eps", [P, 5, TT])
        rstd = keep("rstd", [P, 5, TT])
        neg_half = keep("neg_half", [P, 1])
        ln_stats = keep("ln_stats", [P, TT, 2, 6])
        ln_mv = keep("ln_mv", [P, TT, 2])
        row_max = keep("row_max", [P, QPK])
        neg_m = keep("neg_m", [P, QPK])
        sink_m = keep("sink_m", [P, QPK])
        sink_e = keep("sink_e", [P, QPK])
        denom = keep("denom", [P, QPK])
        denom2 = keep("denom2", [P, QPK])
        r_denom = keep("r_denom", [P, QPK])

        def group(stack, spec):
            return [stack.enter_context(nc.sbuf_tensor(n, s, d)) for n, s, d in spec]

        with ExitStack() as a:
            actA_hi, actA_lo = group(a, [("actA_hi", [P, KT, S], F32R), ("actA_lo", [P, KT, S], F32R)])
        with ExitStack() as a:
            ff_sum, g_ff_post, relu_b, sq_b, junk_ff = group(a, [
                ("ff_sum", [P, TT, D], F32), ("g_ff_post", [P, D], F32), ("relu_b", [P, 2, S], F32),
                ("sq_b", [P, 2, S], F32), ("junk_ff", [P, D], F32)])
        ctx.enter_context(nc.sbuf_tensor("region_a", [P, 2 * KT * S], F32))
        with ExitStack() as a:
            kT_hi, kT_lo, v_hi, v_lo, gates, scores_sb, probs, pT_hi, pT_lo = group(a, [
                ("kT_hi", [P, NKV, S], F32R), ("kT_lo", [P, NKV, S], F32R),
                ("v_hi", [P, TT, NKV, 2 * HD], F32R), ("v_lo", [P, TT, NKV, 2 * HD], F32R),
                ("gates", [P, 2 * KT, S], F32), ("scores_sb", [P, QPK, 2 * P], F32),
                ("probs", [P, QPK, 2 * P], F32), ("pT_hi", [P, 2, QPK * P], F32R),
                ("pT_lo", [P, 2, QPK * P], F32R)])
        with ExitStack() as a:
            x0, _, _, qk = group(a, [
                ("x0", [P, TT, D], F32), ("pad0", [P, 4096], F32), ("pad1", [P, GATES_AHEAD, S], F32),
                ("qk", [P, TT, NH, HD], F32)])
            rot = [None] * 4
            rot[0], rot[1], rot[2], rot[3] = group(a, [(f"rot{i}", [P, TT, NQ, ROT], F32) for i in range(4)])
        with ExitStack() as a:
            v_sgu, ln_g, ln_b, b_s, w_s, _, u_sb = group(a, [
                ("v_sgu", [P, TT, D], F32), ("ln_g", [P, D], F32), ("ln_b", [P, D], F32),
                ("b_s", [P, GROUPS, P], F32), ("w_s", [P, GROUPS, P], F32),
                ("pad2", [P, 2 * KT, S], F32), ("u_sb", [P, KT, S], F32)])
        with ExitStack() as a:
            x1, ff_hi, ff_lo = group(a, [
                ("x1", [P, TT, D], F32), ("ff_hi", [P, HALF_K, S], F32R), ("ff_lo", [P, HALF_K, S], F32R)])
        with ExitStack() as a:
            _, mix = group(a, [("pad3", [P, 16384], F32), ("mix", [P, TT, D], F32)])
        ctx.enter_context(nc.sbuf_tensor("region_b", [P, 20480], F32))

        acc = ctx.enter_context(nc.psum_tensor("acc", [P, 4, COL], F32))
        aux = ctx.enter_context(nc.psum_tensor("aux", [P, 4, COL], F32))

        x_in = [sem(f"x_in{t}") for t in range(TT)]
        consts_in = sem("consts_in")
        sgu_in = sem("sgu_in")
        x_again = sem("x_again")
        g_ff_in = sem("g_ff_in")
        w_loaded = [sem(f"w_loaded{j}") for j in range(SLOTS)]
        stored = sem("stored")
        hi_made, lo_made = sem("hi_made"), sem("lo_made")
        pe_done, acc_to_act, acc_to_dve = sem("pe_done"), sem("acc_to_act"), sem("acc_to_dve")
        pool_consts = sem("pool_consts")
        rstd_made = sem("rstd_made")
        w_mix_made = sem("w_mix_made")
        ff_zeroed = sem("ff_zeroed")
        ssq_dve, ssq_act = sem("ssq_dve"), sem("ssq_act")
        normed = sem("normed")
        turned, turned_hi, turned_lo = sem("turned"), sem("turned_hi"), sem("turned_lo")
        angles, sincos = sem("angles"), sem("sincos")
        rotated = sem("rotated")
        v_hi_made = sem("v_hi_made")
        s_done, s_masked, m_made, p_exp, p_normed = (sem(n) for n in ("s_done", "s_masked", "m_made", "p_exp", "p_normed"))
        pT_done, pT_hi_made, pT_lo_made = sem("pT_done"), sem("pT_hi_made"), sem("pT_lo_made")
        o_done, o_hi_made, o_lo_made = sem("o_done"), sem("o_hi_made"), sem("o_lo_made")
        sig_made, ln_summed = sem("sig_made"), sem("ln_summed")
        ws_turned, ws_copied = sem("ws_turned"), sem("ws_copied")
        ln_var, v_normed = sem("ln_var"), sem("v_normed")
        mix_done, a_made, a_hi, a_lo = sem("mix_done"), sem("a_made"), sem("a_hi"), sem("a_lo")
        merged, merged_hi, merged_lo = sem("merged"), sem("merged_hi"), sem("merged_lo")
        x1_made = sem("x1_made")
        sq_made, ff_hi_made, ff_lo_made = sem("sq_made"), sem("ff_hi_made"), sem("ff_lo_made")
        y_made = sem("y_made")
        dve_step, act_step, pool_step = sem("dve_step"), sem("act_step"), sem("pool_step")

        block = ctx.enter_context(nc.Block())

        def stationary(ring, j):
            return ring[:, j].rearrange("p (k n) -> p k n", k=KT)

        def moving(ring, j):
            return ring[:, j].rearrange("p (k n) -> p k n", n=COL)

        @block.sync
        def _(sp):
            def slot_free(u):
                sp.wait_ge(lo_made, u - SLOTS + 1)

            def load_columns(j, w, col):
                sp.dma_start(stationary(w_raw, j), w[:, 0:KT, col]).then_inc(w_loaded[j], 16)

            def load_rows(j, w, k, col):
                sp.dma_start(moving(w_raw, j), w[:, k:k + 2, col]).then_inc(w_loaded[j], 16)

            for t in range(TT):
                sp.dma_start(x0[:, t], x_v[:, t]).then_inc(x_in[t], 16)
            for j in range(SLOTS):
                load_rows(j, w_in_v, 2 * j, slice(C_Q, C_Q + COL))
            with sp.Fori(1, 3) as b:
                for j in range(SLOTS):
                    slot_free(b * SLOTS + j)
                    load_rows(j, w_in_v, 2 * j, bass.ds(b * COL + C_Q, COL))
            with sp.Fori(0, 4) as i:
                for j in range(SLOTS):
                    slot_free(i * SLOTS + (U_GATE + j))
                    load_columns(j, w_in_v, bass.ds(i * (SLOTS * P) + (C_GATES + j * P), P))
            with sp.Fori(0, 2) as i:
                for j in range(SLOTS):
                    slot_free(i * SLOTS + (U_WB + j))
                    load_columns(j, w_b_v, bass.ds(i * (SLOTS * P) + j * P, P))
            sp.wait_ge(o_done, STEPS)
            sp.dma_start(ln_g[:], ln_v_gain[0:1, :].to_broadcast([P, D])).then_inc(sgu_in, 16)
            sp.dma_start(ln_b[:], ln_v_bias[0:1, :].to_broadcast([P, D])).then_inc(sgu_in, 16)
            sp.dma_start(b_s[:], b_spatial[0:1].to_broadcast([P, GROUPS, P])).then_inc(sgu_in, 16)
            sp.dma_start(w_s[:], w_spatial[0].rearrange("g t s -> t g s")).then_inc(sgu_in, 16)
            with sp.Fori(0, 2) as b:
                for j in range(SLOTS):
                    slot_free(b * SLOTS + (U_VSGU + j))
                    load_rows(j, w_in_v, 2 * j, bass.ds(b * COL + C_V, COL))
            with sp.Fori(0, 2) as i:
                for j in range(SLOTS):
                    slot_free(i * SLOTS + (U_U + j))
                    load_columns(j, w_in_v, bass.ds(i * (SLOTS * P) + (C_U + j * P), P))
            with sp.Fori(0, 2) as i:
                for j in range(SLOTS):
                    slot_free(i * SLOTS + (U_WA + j))
                    load_columns(j, w_a_v, bass.ds(i * (SLOTS * P) + j * P, P))
            sp.wait_ge(mix_done, GROUPS)
            sp.dma_start(x1[:], x_v[:, :, :]).then_inc(x_again, 16)
            with sp.Fori(0, 2) as b:
                for j in range(SLOTS):
                    slot_free(b * SLOTS + (U_WO + j))
                    load_rows(j, w_o_v, 2 * j, bass.ds(b * COL, COL))
            for c in range(2):
                first = U_FF + c * U_HALF
                with sp.Fori(0, HALF_K // SLOTS) as i:
                    for j in range(SLOTS):
                        slot_free(i * SLOTS + (first + j))
                        load_columns(j, w_ff_in_v, bass.ds(i * (SLOTS * P) + (c * HALF_K + j) * P, P))
                if c == 0:
                    sp.wait_ge(pe_done, UNIT_DONE[U_FF - 1])
                    sp.dma_start(g_ff_post[:], norm_ff_post[0:1, :].to_broadcast([P, D])).then_inc(g_ff_in, 16)
                with sp.Fori(0, 2) as h:
                    for n in range(HALF_K // 2):
                        slot_free(h * (HALF_K // 2) + (first + HALF_K + n))
                        load_rows(n % SLOTS, w_ff_out_v, c * HALF_K + 2 * n, bass.ds(h * COL, COL))
            for t in range(TT):
                sp.wait_ge(y_made, t + 1)
                sp.dma_start(out_v[:, t], ff_sum[:, t]).then_inc(stored, 16)
            sp.wait_ge(stored, 16 * TT)

        @block.gpsimd
        def _(pool):
            steps = [0]

            def after(ins):
                steps[0] += 1
                ins.then_inc(pool_step, 1)
                pool.wait_ge(pool_step, steps[0])

            after(nc.gpsimd.memset(neg_half[:], -0.5))
            after(nc.gpsimd.memset(ident[:], 0.0))
            nc.gpsimd.affine_select(out=ident[:], in_=ident[:], compare_op=ALU.not_equal, fill=1.0, base=0,
                                    pattern=[[-1, P]], channel_multiplier=1).then_inc(pool_consts, 1)

            def inv_sqrt(sums, norm, t, scale):
                after(nc.gpsimd.tensor_scalar(var_eps[:, norm, t:t + 1], sums, scale, EPS, ALU.mult, ALU.add))
                nc.gpsimd.tensor_tensor(rstd[:, norm, t:t + 1], var_eps[:, norm, t:t + 1], neg_half[:],
                                        ALU.pow).then_inc(rstd_made, 1)

            for t in range(TT):
                pool.wait_ge(ssq_act if t % 2 else ssq_dve, t // 2 + 1)
                inv_sqrt(ssq[:, 0, t:t + 1], 0, t, 1.0 / D)
            for i in range(ROT):
                last = nc.gpsimd.memset(inv_freq[:, i:i + 1], INV_FREQ[i])
            last.then_inc(pool_consts, 1)
            after(nc.gpsimd.memset(mask[:], 0.0))
            after(nc.gpsimd.affine_select(out=mask[:], in_=mask[:], compare_op=ALU.is_gt, fill=NEG, base=0,
                                          pattern=[[1, 2 * P]], channel_multiplier=-1))
            nc.gpsimd.affine_select(out=mask[:], in_=mask[:], compare_op=ALU.is_ge, fill=NEG, base=P,
                                    pattern=[[-1, 2 * P]], channel_multiplier=1).then_inc(pool_consts, 1)
            for t in range(TT):
                pool.wait_ge(ln_var, t + 1)
                inv_sqrt(ln_mv[:, t, 1:2], 1, t, 1.0)
            pool.wait_ge(ws_copied, 2)
            nc.gpsimd.affine_select(out=w_mix[:], in_=w_mix[:], compare_op=ALU.is_ge, fill=0.0, base=0,
                                    pattern=[[0, GROUPS], [1, P]], channel_multiplier=-1).then_inc(w_mix_made, 1)
            for n, (norm, t) in enumerate(NORM_ORDER):
                pool.wait_ge(ssq_act, 2 + n + 1)
                inv_sqrt(ssq[:, norm - 1, t:t + 1], norm, t, 1.0 / D)
            pool.wait_ge(pe_done, UNIT_DONE[U_FF - 1])
            nc.gpsimd.memset(ff_sum[:], 0.0).then_inc(ff_zeroed, 1)
            for t in range(TT):
                pool.wait_ge(ssq_act, 2 + 2 * TT + TT + t + 1)
                after(nc.gpsimd.tensor_tensor(ssq2[:, t:t + 1], ssq2[:, t:t + 1], ssq[:, 3, t:t + 1], ALU.add))
                inv_sqrt(ssq2[:, t:t + 1], 4, t, 1.0 / D)

        @block.scalar
        def _(act):
            def round_unit(j, loads, used):
                act.wait_ge(w_loaded[j], loads)
                if used is not None:
                    act.wait_ge(pe_done, used)
                nc.scalar.activation(w_hi[:, j], w_raw[:, j], ACT.Copy).then_inc(hi_made, 1)

            def hi_of(u):
                round_unit(u % SLOTS, 16 * (u // SLOTS + 1), UNIT_DONE[u - SLOTS] if u >= SLOTS else None)

            def hi_after(i, u, per=SLOTS):
                counts = UNIT_DONE[u + per] - UNIT_DONE[u]
                round_unit(u % SLOTS, i * (16 * per // SLOTS) + 16 * (u // SLOTS + 2), i * counts + UNIT_DONE[u])

            act.dma_start(g_pre[:], norm_mix_pre[0].rearrange("(k p) -> p k", p=P),
                          allow_slow_non_contiguous=True).then_inc(consts_in, 16)
            act.dma_start(pos_i[:], pos_v, allow_slow_non_contiguous=True).then_inc(consts_in, 16)
            act.dma_start(g_ff_pre[:], norm_ff_pre[0].rearrange("(k p) -> p k", p=P),
                          allow_slow_non_contiguous=True).then_inc(consts_in, 16)
            act.dma_start(sink_b[:], sinks[0:1, :].to_broadcast([P, NQ])).then_inc(consts_in, 16)
            act.dma_start(g_mix_post[:], norm_mix_post[0:1, :].to_broadcast([P, D])).then_inc(consts_in, 16)

            def turned_bank(k):
                return acc[:, k] if k < 4 else aux[:, k - 4]

            for t in (1, 3):
                act.wait_ge(x_in[t], 16)
                if t > 1:
                    act.wait_ge(ssq_act, t // 2)
                nc.scalar.activation(probs[:].rearrange("p h k -> p (h k)"), x0[:, t], ACT.Square,
                                     accum_out=ssq[:, 0, t:t + 1]).then_inc(ssq_act, 1)
            act.wait_ge(consts_in, 80)
            for k in range(KT):
                if k % 2 == 0:
                    hi_of(k // 2)
                act.wait_ge(turned, k + 1)
                nc.scalar.activation(actA_hi[:, k], turned_bank(k), ACT.Copy,
                                     scale=g_pre[:, k:k + 1]).then_inc(turned_hi, 1)
            act.wait_ge(angles, 2)
            nc.scalar.activation(sin_t[:], sin_arg[:], ACT.Sin).then_inc(sincos, 1)
            nc.scalar.activation(cos_t[:], cos_arg[:], ACT.Sin).then_inc(sincos, 1)

            with act.Fori(0, 2) as b:
                for j in range(SLOTS):
                    if j == SLOTS - 1:
                        for t in range(TT):
                            act.wait_ge(pe_done, b * BLOCK_COUNTS + BANK_DONE[SLOTS - 1, t])
                            nc.scalar.activation(qk[:, t, bass.ds(b * 8, 8), :],
                                                 acc[:, t].rearrange("p (h d) -> p h d", d=HD),
                                                 ACT.Copy, scale=HD ** -0.5).then_inc(acc_to_act, 1)
                    hi_after(b, U_QKV + j)
            for j in range(SLOTS):
                if j == SLOTS - 1:
                    for t in range(TT):
                        act.wait_ge(pe_done, BANK_DONE[U_GATE - 1, t])
                        kv = acc[:, t].rearrange("p (c g d) -> p c g d", c=2, d=HD)
                        nc.scalar.activation(qk[:, t, NQ:NH].rearrange("p (g r) d -> p g r d", r=2),
                                             kv[:, 0].unsqueeze(2).to_broadcast([P, NKV, 2, HD]), ACT.Copy)
                        nc.scalar.activation(v_hi[:, t].rearrange("p g (r d) -> p g r d", r=2),
                                             kv[:, 1].unsqueeze(2).to_broadcast([P, NKV, 2, HD]),
                                             ACT.Copy).then_inc(v_hi_made, 1)
                hi_of(2 * SLOTS + j + SLOTS)

            def gate_out(n):
                act.wait_ge(pe_done, UNIT_DONE[U_GATE + n])
                nc.scalar.activation(gates[:, n], acc[:, n % 2], ACT.Copy).then_inc(acc_to_act, 1)
                hi_of(U_GATE + n + SLOTS)

            for n in range(GATES_AHEAD):
                gate_out(n)
                for k in range(4 * n, min(4 * n + 4, KT + NKV)):
                    act.wait_ge(turned, KT + k + 1)
                    dst = actB_hi[:, k] if k < KT else kT_hi[:, k - KT]
                    nc.scalar.activation(dst, aux[:, k % 4], ACT.Copy).then_inc(turned_hi, 1)

            for slot in range(SLOT_COUNT):
                for n in gates_finished(slot):
                    gate_out(n)
                if slot >= 2:
                    s = slot - 2
                    b, g = divmod(s, NKV)
                    act.wait_ge(o_done, s + 1)
                    for f in range(2):
                        half = slice(HD * f, HD * f + HD)
                        src = acc[half, 2 + s % 2, 2 * P * f:2 * P * (f + 1)].rearrange("p (m q) -> p m q", m=2)
                        nc.scalar.activation(actB_hi[half, 2 * g:2 * g + 2, P * b:P * b + P], src,
                                             ACT.Copy).then_inc(o_hi_made, 1)
                if 1 <= slot <= STEPS:
                    s = slot - 1
                    lo = 1 if s < NKV else 0
                    act.wait_ge(pT_done, s + 1)
                    nc.scalar.activation(pT_hi[:, lo:2], aux[:, 2 + lo:4], ACT.Copy).then_inc(pT_hi_made, 1)
                if slot < STEPS:
                    s = slot
                    off = P if s < NKV else 0
                    act.wait_ge(m_made, s + 1)
                    for h in range(QPK):
                        nc.scalar.activation(probs[:, h, off:], scores_sb[:, h, off:], ACT.Exp,
                                             bias=neg_m[:, h:h + 1], accum_out=denom[:, h:h + 1])
                    nc.scalar.activation(sink_e[:], sink_m[:], ACT.Exp).then_inc(p_exp, 1)

            for q in (2, 3, 0, 1):
                part = gates[:, 4 * q:4 * q + 4]
                if q == 2:
                    act.wait_ge(acc_to_act, 2 * TT + 16)
                nc.scalar.activation(part, part, ACT.Sigmoid).then_inc(sig_made, 1)
            with act.Fori(0, 2) as i:
                for j in range(SLOTS):
                    hi_after(i, U_WB + j)
            with act.Fori(0, 2) as b:
                for j in range(SLOTS):
                    if j == SLOTS - 1:
                        for t in range(TT):
                            act.wait_ge(pe_done, b * BLOCK_COUNTS + BANK_DONE[U_VSGU + SLOTS - 1, t])
                            nc.scalar.activation(v_sgu[:, t, bass.ds(b * COL, COL)], acc[:, t],
                                                 ACT.Gelu_apprx_tanh).then_inc(acc_to_act, 1)
                    hi_after(b, U_VSGU + j)
            for n in range(KT):
                act.wait_ge(pe_done, UNIT_DONE[U_U + n])
                nc.scalar.activation(u_sb[:, n], acc[:, n % 4], ACT.Gelu_apprx_tanh).then_inc(acc_to_act, 1)
                if n == 0:
                    for h in range(2):
                        act.wait_ge(ws_turned, h + 1)
                        nc.scalar.activation(w_mix[:, 4 * h:4 * h + 4], aux[:, h].rearrange("p (g t) -> p g t", g=4),
                                             ACT.Copy).then_inc(ws_copied, 1)
                hi_of(U_U + n + SLOTS)
                for g in mix_groups_after(n):
                    act.wait_ge(a_made, g + 1)
                    nc.scalar.activation(actB_hi[:, g], u_sb[:, g], ACT.Copy).then_inc(a_hi, 1)
            with act.Fori(0, 2) as i:
                for j in range(SLOTS):
                    act.wait_ge(merged, i * SLOTS + (j + 1))
                    nc.scalar.activation(actA_hi[:, bass.ds(i * SLOTS + j, 1)].rearrange("p k s -> p (k s)"),
                                         gates[:, bass.ds(i * SLOTS + j, 1)].rearrange("p k s -> p (k s)"),
                                         ACT.Copy).then_inc(merged_hi, 1)
                    hi_after(i, U_WA + j)

            def mix_out(b, t):
                act.wait_ge(pe_done, BANK_DONE[U_WO + (b + 1) * SLOTS - 1, t])
                nc.scalar.activation(mix[:, t, b * COL:(b + 1) * COL], acc[:, t], ACT.Copy).then_inc(acc_to_act, 1)

            for j in range(SLOTS):
                if j == SLOTS - 1:
                    for t in range(TT):
                        mix_out(0, t)
                hi_of(U_WO + SLOTS + j)
            for n, (norm, t) in enumerate(NORM_ORDER):
                if norm == 2:
                    mix_out(1, t)
                    act.wait_ge(acc_to_act, 44 + t + 1)
                    src = mix[:, t]
                else:
                    act.wait_ge(x1_made, t + 1)
                    src = x1[:, t]
                act.wait_ge(ssq_act, 2 + n)
                nc.scalar.activation(ln_g[:], src, ACT.Square,
                                     accum_out=ssq[:, norm - 1, t:t + 1]).then_inc(ssq_act, 1)
            for k in range(KT):
                if k < SLOTS:
                    hi_of(U_FF + k)
                act.wait_ge(turned, KT + KT + NKV + k + 1)
                nc.scalar.activation(actB_hi[:, k], turned_bank(k ^ 4), ACT.Copy,
                                     scale=g_ff_pre[:, k:k + 1]).then_inc(turned_hi, 1)

            for c in range(2):
                first = U_FF + c * U_HALF
                with act.Fori(0, HALF_K // SLOTS) as i:
                    for j in range(SLOTS):
                        act.wait_ge(pe_done, i * SLOTS + UNIT_DONE[first + j])
                        nc.scalar.activation(relu_b[:, j % 2], acc[:, j], ACT.Relu).then_inc(acc_to_act, 1)
                        hi_after(i, first + j)
                        act.wait_ge(sq_made, i * SLOTS + (c * HALF_K + j + 1))
                        nc.scalar.activation(ff_hi[:, bass.ds(i * SLOTS + j, 1)].rearrange("p k s -> p (k s)"),
                                             sq_b[:, j % 2], ACT.Copy).then_inc(ff_hi_made, 1)
                if c == 0:
                    with act.Fori(0, 2) as h:
                        for n in range(HALF_K // 2):
                            hi_after(h, first + HALF_K + n, HALF_K // 2)
                else:
                    for n in range(HALF_K // 2):
                        hi_of(first + HALF_K + SLOTS + n)
                    for h in range(2):
                        for t in range(TT):
                            act.wait_ge(acc_to_dve, 28 + h * TT + t + 1)
                            act.wait_ge(ssq_act, 2 + 2 * TT + h * TT + t)
                            nc.scalar.activation(junk_ff[:, 0:COL], ff_sum[:, t, h * COL:(h + 1) * COL], ACT.Square,
                                                 accum_out=(ssq[:, 3, t:t + 1] if h else ssq2[:, t:t + 1])
                                                 ).then_inc(ssq_act, 1)
                        if h == 0:
                            for j in range(SLOTS):
                                hi_of(UNITS - SLOTS + j)

        @block.vector
        def _(dve):
            steps = [0]

            def after(ins):
                steps[0] += 1
                ins.then_inc(dve_step, 1)
                dve.wait_ge(dve_step, steps[0])

            def lo_of(u, j):
                dve.wait_ge(hi_made, u + 1)
                nc.vector.tensor_tensor(w_lo[:, j], w_raw[:, j], w_hi[:, j].bitcast(F32),
                                        ALU.subtract).then_inc(lo_made, 1)

            def turned_bank(k):
                return acc[:, k] if k < 4 else aux[:, k - 4]

            for t in (0, 2):
                dve.wait_ge(x_in[t], 16)
                if t:
                    dve.wait_ge(ssq_dve, t // 2)
                nc.vector.tensor_tensor_reduce(scores_sb[:].rearrange("p h k -> p (h k)"), x0[:, t], x0[:, t],
                                               1.0, 0.0, ALU.mult, ALU.add, ssq[:, 0, t:t + 1]).then_inc(ssq_dve, 1)
            for t in range(TT):
                dve.wait_ge(rstd_made, t + 1)
                nc.vector.tensor_scalar(x0[:, t], x0[:, t], rstd[:, 0, t:t + 1], None, ALU.mult).then_inc(normed, 1)
            dve.wait_ge(consts_in, 80)
            for k in range(KT):
                if k % 2 == 0:
                    lo_of(k // 2, k // 2)
                dve.wait_ge(turned_hi, k + 1)
                nc.vector.scalar_tensor_tensor(actA_lo[:, k], turned_bank(k), g_pre[:, k:k + 1],
                                               actA_hi[:, k].bitcast(F32), ALU.mult,
                                               ALU.subtract).then_inc(turned_lo, 1)

            def stt(o, a, s, b, op0=ALU.mult, op1=ALU.add):
                after(nc.vector.scalar_tensor_tensor(o, a, s, b, op0, op1))

            def ts(o, a, s1, s2, op0, op1=ALU.bypass):
                if s2 is None:
                    after(nc.vector.tensor_scalar(o, a, s1, None, op0))
                else:
                    after(nc.vector.tensor_scalar(o, a, s1, s2, op0, op1))

            dve.wait_ge(pool_consts, 2)
            after(nc.vector.tensor_copy(pos_f[:], pos_i[:]))
            after(nc.vector.tensor_tensor(ang[:], pos_f[:].unsqueeze(2).to_broadcast([P, TT, ROT]),
                                          inv_freq[:].unsqueeze(1).to_broadcast([P, TT, ROT]), ALU.mult))
            ts(turns[:], ang[:], 1.0 / (2 * np.pi), ROUND, ALU.mult, ALU.add)
            ts(turns[:], turns[:], -ROUND, None, ALU.add)
            ts(turns_hi[:], turns[:], 2.0 ** -12, ROUND, ALU.mult, ALU.add)
            ts(turns_hi[:], turns_hi[:], -ROUND, 2.0 ** 12, ALU.add, ALU.mult)
            after(nc.vector.tensor_tensor(turns[:], turns[:], turns_hi[:], ALU.subtract))
            for part in TWO_PI:
                stt(ang[:], turns_hi[:], -part, ang[:])
                stt(ang[:], turns[:], -part, ang[:])
            for arg, shift in ((sin_arg, 0.0), (cos_arg, np.pi / 2)):
                ts(arg[:], ang[:], float(shift), None, ALU.add)
                ts(turns[:], arg[:], 1.0 / (2 * np.pi), ROUND, ALU.mult, ALU.add)
                ts(turns[:], turns[:], -ROUND, None, ALU.add)
                stt(arg[:], turns[:], -float(np.float32(2 * np.pi)), arg[:])
                stt(arg[:], turns[:], float(np.float32(2 * np.pi)) - 2 * np.pi, arg[:])
                nc.vector.tensor_scalar(arg[:], arg[:], -PI32, PI32, ALU.max, ALU.min).then_inc(angles, 1)
            after(nc.vector.tensor_scalar(neg_sink[:], sink_b[:], -1.0, None, ALU.mult))

            with dve.Fori(0, 2) as b:
                for j in range(SLOTS):
                    lo_of(b * SLOTS + (SLOTS + j), j)

            def rotate(h0, h1):
                n = h1 - h0
                r1, r2 = qk[:, :, h0:h1, 0:ROT], qk[:, :, h0:h1, ROT:2 * ROT]
                c = cos_t[:].unsqueeze(2).to_broadcast([P, TT, n, ROT])
                s = sin_t[:].unsqueeze(2).to_broadcast([P, TT, n, ROT])
                x1c, x2s, x2c, x1s = (r[:, :, 0:n] for r in rot)
                if h0:
                    dve.wait_ge(rotated, 1)
                nc.vector.tensor_tensor(x1c, r1, c, ALU.mult)
                nc.vector.tensor_tensor(x2s, r2, s, ALU.mult)
                nc.vector.tensor_tensor(x2c, r2, c, ALU.mult)
                after(nc.vector.tensor_tensor(x1s, r1, s, ALU.mult))
                nc.vector.tensor_tensor(r1, x1c, x2s, ALU.subtract)
                nc.vector.tensor_tensor(r2, x2c, x1s, ALU.add).then_inc(rotated, 1)

            lo_of(3 * SLOTS, 0)
            dve.wait_ge(sincos, 2)
            dve.wait_ge(acc_to_act, 2 * TT)
            rotate(0, NQ)
            lo_of(3 * SLOTS + 1, 1)
            lo_of(3 * SLOTS + 2, 2)
            for t in range(TT):
                dve.wait_ge(v_hi_made, t + 1)
                v_own = acc[:, t, 2 * P:4 * P].rearrange("p (g d) -> p g d", d=HD)
                for r in range(2):
                    last = nc.vector.tensor_tensor(v_lo[:, t, :, r * HD:(r + 1) * HD], v_own,
                                                   v_hi[:, t, :, r * HD:(r + 1) * HD].bitcast(F32), ALU.subtract)
                last.then_inc(acc_to_dve, 1)
            rotate(NQ, NH)
            lo_of(3 * SLOTS + 3, 3)

            for n in range(GATES_AHEAD):
                for k in range(4 * n, min(4 * n + 4, KT + NKV)):
                    dve.wait_ge(turned_hi, KT + k + 1)
                    hi, dst = (actB_hi[:, k], actB_lo[:, k]) if k < KT else (kT_hi[:, k - KT], kT_lo[:, k - KT])
                    nc.vector.tensor_tensor(dst, aux[:, k % 4], hi.bitcast(F32), ALU.subtract).then_inc(turned_lo, 1)
                lo_of(U_GATE + n + SLOTS, n)

            dve.wait_ge(pool_consts, 3)
            for slot in range(SLOT_COUNT):
                for n in gates_finished(slot):
                    lo_of(U_GATE + n + SLOTS, n % SLOTS)
                if slot >= 2:
                    s = slot - 2
                    b, g = divmod(s, NKV)
                    dve.wait_ge(o_hi_made, 2 * s + 2)
                    for f in range(2):
                        half = slice(HD * f, HD * f + HD)
                        src = acc[half, 2 + s % 2, 2 * P * f:2 * P * (f + 1)].rearrange("p (m q) -> p m q", m=2)
                        at = (half, slice(2 * g, 2 * g + 2), slice(P * b, P * b + P))
                        last = nc.vector.tensor_tensor(actB_lo[at], src, actB_hi[at].bitcast(F32), ALU.subtract)
                    last.then_inc(o_lo_made, 1)
                if slot < STEPS:
                    s = slot
                    g = s % NKV
                    off = P if s < NKV else 0
                    dve.wait_ge(s_done, s + 1)
                    for h in range(QPK):
                        f, m = divmod(h, 2)
                        last = nc.vector.tensor_tensor_reduce(
                            scores_sb[:, h, off:], aux[:, f, 2 * P * m + off:2 * P * (m + 1)], mask[:, off:],
                            1.0, -3e38, ALU.add, ALU.max, row_max[:, h:h + 1])
                    last.then_inc(s_masked, 1)
                    dve.wait_ge(s_masked, s + 1)
                    heads = slice(QPK * g, QPK * (g + 1))
                    by_half = lambda a: a[:, heads].rearrange("p (m f) -> p f m", f=2)
                    v2 = lambda a: a[:].rearrange("p (f m) -> p f m", f=2)
                    after(nc.vector.scalar_tensor_tensor(v2(neg_m), v2(row_max), -1.0, by_half(neg_sink),
                                                         ALU.mult, ALU.min))
                    nc.vector.tensor_tensor(v2(sink_m), by_half(sink_b), v2(neg_m), ALU.add).then_inc(m_made, 1)
                if 1 <= slot <= STEPS:
                    s = slot - 1
                    lo = 1 if s < NKV else 0
                    dve.wait_ge(pT_hi_made, s + 1)
                    nc.vector.tensor_tensor(pT_lo[:, lo:2], aux[:, 2 + lo:4], pT_hi[:, lo:2].bitcast(F32),
                                            ALU.subtract).then_inc(pT_lo_made, 1)
                if slot < STEPS:
                    s = slot
                    dve.wait_ge(p_exp, s + 1)
                    after(nc.vector.tensor_tensor(denom2[:], denom[:], sink_e[:], ALU.add))
                    after(nc.vector.reciprocal(r_denom[:], denom2[:]))
                    for h in range(QPK):
                        last = nc.vector.tensor_scalar(probs[:, h, off:], probs[:, h, off:], r_denom[:, h:h + 1],
                                                       None, ALU.mult)
                    last.then_inc(p_normed, 1)

            with dve.Fori(0, 2) as i:
                for j in range(SLOTS):
                    own = gates[:, bass.ds(i * SLOTS + (KT + j), 1)].rearrange("p k s -> p (k s)")
                    dve.wait_ge(sig_made, i + 1)
                    dve.wait_ge(pe_done, i * SLOTS + UNIT_DONE[U_WB + j])
                    nc.vector.tensor_tensor(own, acc[:, j], own, ALU.mult).then_inc(acc_to_dve, 1)
                    lo_of(i * SLOTS + (U_WB + SLOTS + j), j)
            for b in range(2):
                for j in range(SLOTS):
                    lo_of(U_VSGU + (b + 1) * SLOTS + j, j)
                for t in range(TT):
                    dve.wait_ge(acc_to_act, 24 + b * TT + t + 1)
                    nc.vector.bn_stats(ln_stats[:, t, b], v_sgu[:, t, b * COL:(b + 1) * COL]).then_inc(ln_summed, 1)
            dve.wait_ge(ln_summed, 2 * TT)
            for t in range(TT):
                nc.vector.bn_aggr(ln_mv[:, t], ln_stats[:, t]).then_inc(ln_var, 1)
            dve.wait_ge(sgu_in, 64)

            def layer_norm(t):
                dve.wait_ge(rstd_made, TT + t + 1)
                dve.wait_ge(ln_var, t + 1)
                after(nc.vector.tensor_scalar(v_sgu[:, t], v_sgu[:, t], ln_mv[:, t, 0:1], rstd[:, 1, t:t + 1],
                                              ALU.subtract, ALU.mult))
                after(nc.vector.tensor_tensor(v_sgu[:, t], v_sgu[:, t], ln_g[:], ALU.mult))
                nc.vector.tensor_tensor(v_sgu[:, t], v_sgu[:, t], ln_b[:], ALU.add).then_inc(v_normed, 1)

            for n in range(KT):
                if n < 2:
                    layer_norm(2 * n)
                    layer_norm(2 * n + 1)
                lo_of(U_U + n + SLOTS, n % SLOTS)
                for g in mix_groups_after(n):
                    bias = b_s[:, g].unsqueeze(1).to_broadcast([P, TT, P])
                    mixed = aux[:, g % 4].rearrange("p (c t) -> p c t", t=P)
                    tmp = w_s[:, TT * (g % 2):TT * (g % 2 + 1)]
                    dve.wait_ge(mix_done, g + 1)
                    after(nc.vector.tensor_tensor(tmp, mixed, bias, ALU.add))
                    dve.wait_ge(acc_to_act, 32 + g + 1)
                    u_g = u_sb[:, g].rearrange("p (c t) -> p c t", t=P)
                    nc.vector.tensor_tensor(u_g, u_g, tmp, ALU.mult).then_inc(a_made, 1)
                    dve.wait_ge(a_hi, g + 1)
                    nc.vector.tensor_tensor(actB_lo[:, g], u_sb[:, g], actB_hi[:, g].bitcast(F32),
                                            ALU.subtract).then_inc(a_lo, 1)
            dve.wait_ge(sig_made, 4)
            with dve.Fori(0, 2) as i:
                for j in range(SLOTS):
                    at = lambda k0: gates[:, bass.ds(i * SLOTS + (k0 + j), 1)].rearrange("p k s -> p (k s)")
                    dve.wait_ge(pe_done, i * SLOTS + UNIT_DONE[U_WA + j])
                    nc.vector.tensor_tensor(at(0), acc[:, j], at(0), ALU.mult).then_inc(acc_to_dve, 1)
                    dve.wait_ge(acc_to_dve, i * SLOTS + (TT + 8 + j + 1))
                    nc.vector.tensor_tensor(at(0), at(0), at(KT), ALU.add).then_inc(merged, 1)
                    dve.wait_ge(merged_hi, i * SLOTS + (j + 1))
                    dst = bass.ds(i * SLOTS + j, 1)
                    nc.vector.tensor_tensor(actA_lo[:, dst].rearrange("p k s -> p (k s)"), at(0),
                                            actA_hi[:, dst].rearrange("p k s -> p (k s)").bitcast(F32),
                                            ALU.subtract).then_inc(merged_lo, 1)
                    lo_of(i * SLOTS + (U_WA + SLOTS + j), j)
            for j in range(SLOTS):
                lo_of(U_WO + SLOTS + j, j)
            dve.wait_ge(x_again, 16)
            for n, (norm, t) in enumerate(NORM_ORDER):
                dve.wait_ge(rstd_made, 2 * TT + n + 1)
                if norm == 2:
                    dve.wait_ge(ssq_act, 2 + n + 1)
                    after(nc.vector.scalar_tensor_tensor(mix[:, t], mix[:, t], rstd[:, 2, t:t + 1], g_mix_post[:],
                                                         ALU.mult, ALU.mult))
                    nc.vector.tensor_tensor(x1[:, t], mix[:, t], x1[:, t], ALU.add).then_inc(x1_made, 1)
                else:
                    nc.vector.tensor_scalar(mix[:, t], x1[:, t], rstd[:, 3, t:t + 1], None,
                                            ALU.mult).then_inc(normed, 1)
            for k in range(KT):
                if k < SLOTS:
                    lo_of(U_FF + k, k)
                dve.wait_ge(turned_hi, 2 * KT + NKV + k + 1)
                nc.vector.scalar_tensor_tensor(actB_lo[:, k], turned_bank(k ^ 4), g_ff_pre[:, k:k + 1],
                                               actB_hi[:, k].bitcast(F32), ALU.mult,
                                               ALU.subtract).then_inc(turned_lo, 1)
            for c in range(2):
                first = U_FF + c * U_HALF
                relus = 48 + c * HALF_K
                with dve.Fori(0, HALF_K // SLOTS) as i:
                    for j in range(SLOTS):
                        dve.wait_ge(acc_to_act, i * SLOTS + (relus + j + 1))
                        nc.vector.tensor_tensor(sq_b[:, j % 2], relu_b[:, j % 2], relu_b[:, j % 2],
                                                ALU.mult).then_inc(sq_made, 1)
                        lo_of(i * SLOTS + (first + SLOTS + j), j)
                        dve.wait_ge(ff_hi_made, i * SLOTS + (c * HALF_K + j + 1))
                        at = bass.ds(i * SLOTS + j, 1)
                        nc.vector.tensor_tensor(ff_lo[:, at].rearrange("p k s -> p (k s)"), sq_b[:, j % 2],
                                                ff_hi[:, at].rearrange("p k s -> p (k s)").bitcast(F32),
                                                ALU.subtract).then_inc(ff_lo_made, 1)
                if c == 0:
                    dve.wait_ge(ff_zeroed, 1)
                for h in range(2):
                    last_half = c == 1 and h == 1
                    for n in range(HALF_K // 2):
                        u = first + HALF_K + h * (HALF_K // 2) + n + SLOTS
                        if n == HALF_K // 2 - 1 or (last_half and n == SLOTS):
                            for t in range(TT):
                                dve.wait_ge(pe_done, BANK_DONE[first + HALF_K + (h + 1) * (HALF_K // 2) - 1, t])
                                part = ff_sum[:, t, h * COL:(h + 1) * COL]
                                nc.vector.tensor_tensor(part, acc[:, t], part, ALU.add).then_inc(acc_to_dve, 1)
                            if last_half:
                                break
                        lo_of(u, n % SLOTS)
            dve.wait_ge(g_ff_in, 16)
            for t in range(TT):
                dve.wait_ge(rstd_made, 2 * TT + 2 * TT + t + 1)
                after(nc.vector.scalar_tensor_tensor(ff_sum[:, t], ff_sum[:, t], rstd[:, 4, t:t + 1], g_ff_post[:],
                                                     ALU.mult, ALU.mult))
                nc.vector.tensor_tensor(ff_sum[:, t], ff_sum[:, t], x1[:, t], ALU.add).then_inc(y_made, 1)

        @block.tensor
        def _(pe):
            def product(o, a, b, first, last):
                (a_hi, a_lo), (b_hi, b_lo) = a, b
                nc.tensor.matmul(o, a_hi, b_hi, start=first, stop=False)
                nc.tensor.matmul(o, a_hi, b_lo, start=False, stop=False)
                return nc.tensor.matmul(o, a_lo, b_hi, start=False, stop=last)

            def columns_unit(j, acts, bank, ks=range(KT)):
                hi, lo = stationary(w_hi, j), stationary(w_lo, j)
                for k in ks:
                    m = product(acc[:, bank], (hi[:, k], lo[:, k]), (acts[0][:, k], acts[1][:, k]),
                                k == 0, k == KT - 1)
                return m

            def rows_step(j, acts, k0, t, first, last):
                hi, lo = moving(w_hi, j), moving(w_lo, j)
                for q in range(2):
                    at = (slice(None), k0 + q, slice(t * P, (t + 1) * P))
                    m = product(acc[:, t], (acts[0][at], acts[1][at]), (hi[:, q], lo[:, q]),
                                first and q == 0, last and q == 1)
                return m

            def rows_block(acts, first_unit, units=SLOTS, bank_free=None, acts_ready=None):
                for n in range(units):
                    pe.wait_ge(lo_made, first_unit + (n + 1))
                    if acts_ready:
                        acts_ready(n)
                    for t in range(TT):
                        if n == 0 and bank_free:
                            bank_free(t)
                        m = rows_step(n % SLOTS, acts, 2 * n, t, n == 0, n == units - 1)
                        if n == units - 1 or t == TT - 1:
                            m.then_inc(pe_done, 1)

            actA, actB = (actA_hi, actA_lo), (actB_hi, actB_lo)

            def turned_bank(k):
                return acc[:, k] if k < 4 else aux[:, k - 4]

            pe.wait_ge(pool_consts, 1)
            for k in range(KT):
                for t in range(TT):
                    if k == 0:
                        pe.wait_ge(normed, t + 1)
                    m = nc.tensor.transpose(turned_bank(k)[:, t * P:(t + 1) * P], x0[:, t, k * P:(k + 1) * P], ident[:])
                m.then_inc(turned, 1)

            rows_block(actA, U_QKV, bank_free=lambda t: pe.wait_ge(turned_lo, t + 1),
                       acts_ready=lambda n: pe.wait_ge(turned_lo, 2 * n + 2))
            with pe.Fori(1, 3) as b:
                rows_block(actA, b * SLOTS, bank_free=lambda t: pe.wait_ge(acc_to_act, b * TT + (t + 1 - TT)))

            def gate_k(n, k):
                if k == 0:
                    pe.wait_ge(lo_made, U_GATE + n + 1)
                    if n < 2:
                        pe.wait_ge(acc_to_dve, n + 1)
                    else:
                        pe.wait_ge(acc_to_act, 2 * TT + n - 1)
                m = columns_unit(n % SLOTS, actA, n % 2, [k])
                if k == KT - 1:
                    m.then_inc(pe_done, 1)

            for n in range(GATES_AHEAD):
                for k in range(KT):
                    gate_k(n, k)
                for k in range(4 * n, min(4 * n + 4, KT + NKV)):
                    if k == 0:
                        pe.wait_ge(rotated, 1)
                    if k == KT:
                        pe.wait_ge(rotated, 2)
                    if k >= 4:
                        pe.wait_ge(turned_lo, KT + k - 3)
                    for t in range(TT):
                        m = nc.tensor.transpose(aux[:, k % 4, t * P:(t + 1) * P],
                                                qk[:, t, 2 * k:2 * k + 2].rearrange("p h d -> p (h d)"), ident[:])
                    m.then_inc(turned, 1)

            def scores(s):
                b, g = divmod(s, NKV)
                if s == 0:
                    pe.wait_ge(turned_lo, 2 * KT + NKV)
                else:
                    pe.wait_ge(s_masked, s)
                k0 = max(b - 1, 0)
                for m2 in range(2):
                    for f in range(2):
                        half = slice(HD * f, HD * f + HD)
                        q_at = (half, 2 * g + m2, slice(P * b, P * b + P))
                        k_at = (half, g, slice(P * k0, P * b + P))
                        o = aux[:, f, 2 * P * (m2 + 1) - P * (b + 1 - k0):2 * P * (m2 + 1)]
                        m = product(o, (actB_hi[q_at], actB_lo[q_at]), (kT_hi[k_at], kT_lo[k_at]), True, True)
                m.then_inc(s_done, 1)

            def turn_probs(s):
                pe.wait_ge(p_normed, s + 1)
                if s:
                    pe.wait_ge(pT_lo_made, s)
                for kb in range(1 if s < NKV else 0, 2):
                    for h in range(QPK):
                        m = nc.tensor.transpose(aux[:, 2 + kb, P * h:P * h + P], probs[:, h, P * kb:P * kb + P],
                                                ident[:])
                m.then_inc(pT_done, 1)

            def values(s):
                b, g = divmod(s, NKV)
                pe.wait_ge(pT_lo_made, s + 1)
                if s < 2:
                    pe.wait_ge(acc_to_dve, 3 + s)
                else:
                    pe.wait_ge(o_lo_made, s - 1)
                for kb in range(0 if b else 1, 2):
                    m = product(acc[:, 2 + s % 2], (v_hi[:, b - 1 + kb, g], v_lo[:, b - 1 + kb, g]),
                                (pT_hi[:, kb], pT_lo[:, kb]), kb == 0 or b == 0, kb == 1)
                m.then_inc(o_done, 1)

            done = 0
            for slot in range(SLOT_COUNT):
                while done < k_steps_until(slot):
                    gate_k(GATES_AHEAD + done // KT, done % KT)
                    done += 1
                if slot >= 2:
                    values(slot - 2)
                if slot < STEPS:
                    scores(slot)
                if 1 <= slot <= STEPS:
                    turn_probs(slot - 1)

            pe.wait_ge(o_lo_made, STEPS)
            pe.wait_ge(acc_to_act, 2 * TT + 16)
            with pe.Fori(0, 2) as i:
                for j in range(SLOTS):
                    pe.wait_ge(lo_made, i * SLOTS + (U_WB + j + 1))
                    pe.wait_ge(acc_to_dve, i * SLOTS + (j + 1))
                    m = columns_unit(j, actB, j)
                    m.then_inc(pe_done, 1)
            rows_block(actA, U_VSGU, bank_free=lambda t: pe.wait_ge(acc_to_dve, 8 + t + 1))
            rows_block(actA, U_VSGU + SLOTS, bank_free=lambda t: pe.wait_ge(acc_to_act, 24 + t + 1))
            for n in range(KT):
                pe.wait_ge(lo_made, U_U + n + 1)
                pe.wait_ge(acc_to_act, 28 + n + 1)
                m = columns_unit(n % SLOTS, actA, n % 4)
                m.then_inc(pe_done, 1)
                if n == 0:
                    pe.wait_ge(sgu_in, 64)
                    for g in range(GROUPS):
                        m = nc.tensor.transpose(aux[:, g // 4, (g % 4) * P:(g % 4 + 1) * P], w_s[:, g], ident[:])
                        if g % 4 == 3:
                            m.then_inc(ws_turned, 1)
                for g in mix_groups_after(n):
                    if g == 0:
                        pe.wait_ge(w_mix_made, 1)
                        pe.wait_ge(v_normed, TT)
                    if g >= 4:
                        pe.wait_ge(a_made, g - 3)
                    for c in range(TT):
                        m = nc.tensor.matmul(aux[:, g % 4, c * P:(c + 1) * P], v_sgu[:, c, g * P:(g + 1) * P],
                                             w_mix[:, g], start=True, stop=True)
                    m.then_inc(mix_done, 1)
            pe.wait_ge(acc_to_act, 40)
            with pe.Fori(0, 2) as i:
                for j in range(SLOTS):
                    pe.wait_ge(lo_made, i * SLOTS + (U_WA + j + 1))
                    pe.wait_ge(acc_to_dve, i * SLOTS + (8 + j + 1))
                    for k in range(KT):
                        pe.wait_ge(a_lo, k + 1)
                        m = columns_unit(j, actB, j, [k])
                    m.then_inc(pe_done, 1)
            rows_block(actA, U_WO, bank_free=lambda t: pe.wait_ge(acc_to_dve, 16 + t + 1),
                       acts_ready=lambda n: pe.wait_ge(merged_lo, 2 * n + 2))

            def rows_tiles_outside(acts, first_unit, n0, units, bank_free):
                for t in range(TT):
                    bank_free(t)
                    for n in range(n0, units):
                        if t == 0:
                            pe.wait_ge(lo_made, first_unit + n + 1)
                        m = rows_step(n % SLOTS, acts, 2 * n, t, n == 0, n == units - 1)
                        if t == TT - 1 or n == units - 1:
                            m.then_inc(pe_done, 1)

            rows_tiles_outside(actA, U_WO + SLOTS, 0, SLOTS, lambda t: pe.wait_ge(acc_to_act, 40 + t + 1))
            for k in range(KT):
                if k >= 4:
                    pe.wait_ge(acc_to_act, 40 + TT + k - 3)
                for t in range(TT):
                    if k == 0:
                        pe.wait_ge(normed, TT + t + 1)
                    m = nc.tensor.transpose(turned_bank(k ^ 4)[:, t * P:(t + 1) * P], mix[:, t, k * P:(k + 1) * P],
                                            ident[:])
                m.then_inc(turned, 1)
            for c in range(2):
                first = U_FF + c * U_HALF
                relus = 48 + c * HALF_K
                if c == 0:
                    pe.wait_ge(turned_lo, 2 * KT + NKV + 5)
                with pe.Fori(0, HALF_K // SLOTS) as i:
                    for j in range(SLOTS):
                        pe.wait_ge(lo_made, i * SLOTS + (first + j + 1))
                        pe.wait_ge(acc_to_act, i * SLOTS + (relus - SLOTS + j + 1))
                        if c == 1:
                            pe.wait_ge(acc_to_dve, 28 + j + 1 - 4)
                        for k in range(KT):
                            if c == 0:
                                pe.wait_ge(turned_lo, 2 * KT + NKV + max(k + 1, j + 5))
                            m = columns_unit(j, actB, j, [k])
                        m.then_inc(pe_done, 1)
                ff = (ff_hi, ff_lo)
                rows_block(ff, first + HALF_K, units=HALF_K // 2,
                           bank_free=lambda t: pe.wait_ge(acc_to_act, relus + HALF_K - SLOTS + t + 1),
                           acts_ready=lambda n: pe.wait_ge(ff_lo_made, c * HALF_K + 2 * n + 2))
                if c == 0:
                    rows_block(ff, first + HALF_K + HALF_K // 2, units=HALF_K // 2,
                               bank_free=lambda t: pe.wait_ge(acc_to_dve, 20 + t + 1))
                else:
                    last = first + HALF_K + HALF_K // 2
                    for n in range(SLOTS):
                        pe.wait_ge(lo_made, last + n + 1)
                        for t in range(TT):
                            if n == 0:
                                pe.wait_ge(acc_to_dve, 28 + t + 1)
                            m = rows_step(n, ff, 2 * n, t, n == 0, False)
                        m.then_inc(pe_done, 1)
                    rows_tiles_outside(ff, last, SLOTS, HALF_K // 2, lambda t: None)


INPUTS = ["x", "positions", "w_in", "ln_v_gain", "ln_v_bias", "w_spatial", "b_spatial", "sinks", "w_a", "w_b",
          "w_o", "norm_mix_pre", "norm_mix_post", "w_ff_in", "w_ff_out", "norm_ff_pre", "norm_ff_post"]


def kernel(**inputs):
    import concourse.bacc as bacc
    from concourse.bass_utils import run_bass_kernel_spmd

    nc = bacc.Bacc("TRN2", target_bir_lowering=False, num_devices=1)
    arrays, args = {}, []
    for name in INPUTS:
        a = np.ascontiguousarray(inputs[name])
        arrays[f"in_{name}"] = a
        args.append(nc.dram_tensor(f"in_{name}", a.shape, mybir.dt.from_np(a.dtype), kind="ExternalInput").ap())
    result = nc.dram_tensor("out", (1, S, D), F32, kind="ExternalOutput").ap()
    hybrid_block(nc, *args, result)
    r = run_bass_kernel_spmd(nc, [arrays], core_ids=[0])
    return r.results[0]["out"]
```

```python
from contextlib import ExitStack

import numpy as np

import concourse.bass as bass
from concourse import mybir

F32 = mybir.dt.float32
F32R = mybir.dt.float32r
I32 = mybir.dt.int32
ACT = mybir.ActivationFunctionType
ALU = mybir.AluOpType

P = 128
D = 1024
S = 512
TT = S // P
KT = D // P
HD = 64
NQ = D // HD
NKV = NQ // 4
QPK = NQ // NKV
NH = NQ + 2 * NKV
ROT = HD // 4 // 2
GROUPS = 8
FF = 4 * D
IN_W = 3 * D + 2 * NKV * HD + 2 * D
EPS = 1e-6
ROOT_MEAN = D ** -0.5
NEG = -1e30
WARM_UP = 40
SLOTS = 4
UNIT = KT * P
COL = 512

C_U, C_V, C_Q = 0, D, 2 * D
C_KV = C_Q + D
C_GATES = C_KV + 2 * NKV * HD

U_QKV = 0
U_SIDE = U_QKV + 12
SIDE = 3 * KT
U_VSGU = U_SIDE + SIDE
U_WB = U_VSGU + 8
U_WA = U_WB + 8
U_WO = U_WA + 8
U_FF = U_WO + 8
HALF_K = FF // P // 2
U_HALF = 2 * HALF_K
UNITS = U_FF + 2 * U_HALF

def _pe_counts():
    unit_done, bank_done, n = {}, {}, 0

    def columns(first, units):
        nonlocal n
        for u in range(first, first + units):
            n += 1
            unit_done[u] = bank_done[u, 0] = n

    def rows(first, units, inside=SLOTS):
        nonlocal n
        last = first + units - 1
        for u in range(first, min(first + inside, last)):
            n += 1
            unit_done[u] = n
        if inside < units:
            for t in range(TT - 1):
                n += 1
                bank_done[last, t] = n
            for u in range(first + inside, last + 1):
                n += 1
                unit_done[u] = n
            bank_done[last, TT - 1] = n
        else:
            for t in range(TT):
                n += 1
                bank_done[last, t] = n
            unit_done[last] = n

    for b in range(3):
        rows(U_QKV + b * SLOTS, SLOTS)
    columns(U_SIDE, SIDE)
    for b in range(2):
        rows(U_VSGU + b * SLOTS, SLOTS)
    columns(U_WB, KT)
    columns(U_WA, KT)
    rows(U_WO, SLOTS)
    rows(U_WO + SLOTS, SLOTS, inside=0)
    for c in range(2):
        first = U_FF + c * U_HALF
        columns(first, HALF_K)
        rows(first + HALF_K, HALF_K // 2, inside=HALF_K // 2)
        rows(first + HALF_K + HALF_K // 2, HALF_K // 2, inside=SLOTS if c else HALF_K // 2)
    return unit_done, bank_done


UNIT_DONE, BANK_DONE = _pe_counts()
BLOCK_COUNTS = SLOTS - 1 + TT

A_SIDE = 2 * TT
A_VSGU = A_SIDE + SIDE
A_WO = A_VSGU + 2 * TT
A_FF = A_WO + TT
V_KV = 0
V_WB = V_KV + TT
V_WA = V_WB + KT
V_WO = V_WA + KT
V_FF = V_WO + TT
Q_MIX = TT - 1
T_QK = TT
T_FF = T_QK + KT + NKV

SIDE_AHEAD = 4
STEPS = TT * NKV
SLOT_COUNT = STEPS + 2
SIDE_K_STEPS = (SIDE - SIDE_AHEAD) * KT


WO_ORDER = {
    "pool": [("mix", 0), ("x1", 0), ("mix", 1), ("x1", 1), ("mix", 2), ("x1", 2), ("mix", 3), ("x1", 3)],
    "act": [("sq", 0), ("sqx", 0), ("sq", 1), ("sqx", 1), ("turn", 0), ("sq", 2), ("unit", 0), ("turn", 1),
            ("unit", 1), ("sqx", 2), ("sq", 3), ("unit", 2), ("sqx", 3), ("unit", 3), ("turn", 2), ("turn", 3)],
    "dve": [("mix", 0), ("x1", 0), ("norm", 0), ("mix", 1), ("x1", 1), ("norm", 1), ("turn", 0), ("mix", 2),
            ("unit", 0), ("turn", 1), ("x1", 2), ("unit", 1), ("mix", 3), ("x1", 3), ("norm", 2), ("unit", 2),
            ("norm", 3), ("unit", 3), ("turn", 2), ("turn", 3)],
}


def _before(kind, other):
    order = WO_ORDER["act"]
    return [sum(k == other for k, _ in order[:order.index((kind, t))]) for t in range(TT)]


SQX_BEFORE, SQ_BEFORE = _before("sq", "sqx"), _before("sqx", "sq")


def k_steps_until(slot):
    light, heavy, drain = 7, 10, 6
    if slot >= STEPS:
        return SIDE_K_STEPS - (SLOT_COUNT - 1 - slot) * drain
    return light * min(slot + 1, NKV) + heavy * max(slot + 1 - NKV, 0)


def side_finished(slot):
    before = k_steps_until(slot - 1) // KT if slot else 0
    return range(SIDE_AHEAD + before, SIDE_AHEAD + k_steps_until(slot) // KT)


def mix_groups_after(unit):
    return {3: [0, 1], 4: [2, 3], 5: [4, 5], 6: [6, 7]}.get(unit, [])


def _two_pi_parts():
    rest, parts = 2 * np.pi, []
    for low in (-9, -21, -33):
        part = np.floor(rest * 2.0 ** -low) * 2.0 ** low
        parts.append(float(part))
        rest -= part
    return parts + [float(np.float32(rest))]


TWO_PI = _two_pi_parts()
ROUND = 1.5 * 2.0 ** 23
PI32 = 3.1415925
INV_FREQ = [float(np.float32(500000.0 ** (-2 * i / (2 * ROT)))) for i in range(ROT)]


def hybrid_block(nc, x, positions, w_in, ln_v_gain, ln_v_bias, w_spatial, b_spatial, sinks, w_a, w_b,
                 w_o, norm_mix_pre, norm_mix_post, w_ff_in, w_ff_out, norm_ff_pre, norm_ff_post, out):
    x_v = x[0].rearrange("(t p) d -> p t d", p=P)
    out_v = out[0].rearrange("(t p) d -> p t d", p=P)
    pos_v = positions[0].rearrange("(t p) -> p t", p=P)

    def rows(w):
        return w[0].rearrange("(k p) n -> p k n", p=P)

    w_in_v, w_a_v, w_b_v, w_o_v = rows(w_in), rows(w_a), rows(w_b), rows(w_o)
    w_ff_in_v, w_ff_out_v = rows(w_ff_in), rows(w_ff_out)

    with ExitStack() as ctx:
        def sem(name):
            return ctx.enter_context(nc.semaphore(name))

        def keep(name, shape, dt=F32):
            return ctx.enter_context(nc.sbuf_tensor(name, shape, dt))

        w_raw = keep("w_raw", [P, SLOTS, UNIT])
        w_hi = keep("w_hi", [P, SLOTS, UNIT], F32R)
        w_lo = keep("w_lo", [P, SLOTS, UNIT], F32R)
        actB_hi = keep("actB_hi", [P, KT, S], F32R)
        actB_lo = keep("actB_lo", [P, KT, S], F32R)
        ident = keep("ident", [P, P])
        mask = keep("mask", [P, 2 * P])
        pos_i = keep("pos_i", [P, TT], I32)
        pos_f = keep("pos_f", [P, TT])
        inv_freq = keep("inv_freq", [P, ROT])
        ang = keep("ang", [P, TT, ROT])
        turns = keep("turns", [P, TT, ROT])
        turns_hi = keep("turns_hi", [P, TT, ROT])
        sin_arg = keep("sin_arg", [P, TT, ROT])
        cos_arg = keep("cos_arg", [P, TT, ROT])
        sin_t = keep("sin_t", [P, TT, ROT])
        cos_t = keep("cos_t", [P, TT, ROT])
        sink_b = keep("sink_b", [P, NQ])
        neg_sink = keep("neg_sink", [P, NQ])
        ssq = keep("ssq", [P, 6, TT])
        ssq_eps = keep("ssq_eps", [P, 2, TT])
        var_eps = keep("var_eps", [P, 5, TT])
        rstd = keep("rstd", [P, 5, TT])
        neg_half = keep("neg_half", [P, 1])
        ln_stats = keep("ln_stats", [P, TT, 2, 6])
        ln_mv = keep("ln_mv", [P, TT, 2])
        row_max = keep("row_max", [P, QPK])
        neg_m = keep("neg_m", [P, QPK])
        sink_m = keep("sink_m", [P, QPK])
        sink_e = keep("sink_e", [P, QPK])
        denom = keep("denom", [P, QPK])
        denom2 = keep("denom2", [P, QPK])
        r_denom = keep("r_denom", [P, QPK])

        def group(stack, spec):
            return [stack.enter_context(nc.sbuf_tensor(n, s, d)) for n, s, d in spec]

        with ExitStack() as a:
            actA_hi, actA_lo = group(a, [("actA_hi", [P, KT, S], F32R), ("actA_lo", [P, KT, S], F32R)])
        with ExitStack() as a:
            ff_sum, g_ff_post, relu_b, sq_b, junk_ff = group(a, [
                ("ff_sum", [P, TT, D], F32), ("g_ff_post", [P, D], F32), ("relu_b", [P, 2, S], F32),
                ("sq_b", [P, 2, S], F32), ("junk_ff", [P, D], F32)])
        ctx.enter_context(nc.sbuf_tensor("region_a", [P, 2 * KT * S], F32))
        with ExitStack() as a:
            kT_hi, kT_lo, v_pair, o_part, o_sum, scores_sb, gates, probs, pT_hi, pT_lo, u_sb = group(a, [
                ("kT_hi", [P, NKV, S], F32R), ("kT_lo", [P, NKV, S], F32R),
                ("v_pair", [P, TT, NKV, 2 * HD], F32R), ("o_part", [P, 2, 2, P], F32),
                ("o_sum", [P, 2, 2, P], F32), ("scores_sb", [P, QPK, 2 * P], F32),
                ("gates", [P, 2 * KT, S], F32), ("probs", [P, QPK, 2 * P], F32),
                ("pT_hi", [P, 2, QPK * P], F32R), ("pT_lo", [P, 2, QPK * P], F32R),
                ("u_sb", [P, KT, S], F32)])
        with ExitStack() as a:
            x0, _, g_pre, _, qk = group(a, [
                ("x0", [P, TT, D], F32), ("pad0", [P, 4096], F32), ("g_pre", [P, D], F32), ("pad1", [P, D], F32),
                ("qk", [P, TT, NH, HD], F32)])
            rot = [None] * 4
            rot[0], rot[1], rot[2], rot[3] = group(a, [(f"rot{i}", [P, TT, NQ, ROT], F32) for i in range(4)])
        with ExitStack() as a:
            v_sgu, ln_g, ln_b, b_s, w_s, _, w_mix = group(a, [
                ("v_sgu", [P, TT, D], F32), ("ln_g", [P, D], F32), ("ln_b", [P, D], F32),
                ("b_s", [P, GROUPS, P], F32), ("w_s", [P, GROUPS, P], F32),
                ("pad2", [P, 2 * KT, S], F32), ("w_mix", [P, GROUPS, P], F32)])
        with ExitStack() as a:
            x1, = group(a, [("x1", [P, TT, D], F32)])
            with ExitStack() as b:
                junk_wo, g_mix_post, g_ff_pre = group(b, [
                    ("junk_wo", [P, D], F32), ("g_mix_post", [P, D], F32), ("g_ff_pre", [P, D], F32)])
            ff_hi, ff_lo = group(a, [
                ("ff_hi", [P, HALF_K, S], F32R), ("ff_lo", [P, HALF_K, S], F32R)])
        with ExitStack() as a:
            _, mix = group(a, [("pad3", [P, 16384], F32), ("mix", [P, TT, D], F32)])
        ctx.enter_context(nc.sbuf_tensor("region_b", [P, 23552], F32))

        acc = ctx.enter_context(nc.psum_tensor("acc", [P, 4, COL], F32))
        aux = ctx.enter_context(nc.psum_tensor("aux", [P, 4, COL], F32))

        x_in = [sem(f"x_in{t}") for t in range(TT)]
        g_pre_in = sem("g_pre_in")
        consts_in = sem("consts_in")
        wo_in = sem("wo_in")
        ws_in = sem("ws_in")
        sgu_in = sem("sgu_in")
        x_again = sem("x_again")
        g_ff_in = sem("g_ff_in")
        w_loaded = [sem(f"w_loaded{j}") for j in range(SLOTS)]
        stored = sem("stored")
        hi_made, lo_made = sem("hi_made"), sem("lo_made")
        pe_done, acc_to_act, acc_to_dve = sem("pe_done"), sem("acc_to_act"), sem("acc_to_dve")
        pool_consts = sem("pool_consts")
        rstd_made = sem("rstd_made")
        w_mix_made = sem("w_mix_made")
        ff_zeroed = sem("ff_zeroed")
        ssq_dve, ssq_act = sem("ssq_dve"), sem("ssq_act")
        ssq_x1 = sem("ssq_x1")
        half_scaled = sem("half_scaled")
        normed = sem("normed")
        turned, turned_hi, turned_lo = sem("turned"), sem("turned_hi"), sem("turned_lo")
        angles, sincos = sem("angles"), sem("sincos")
        rotated = sem("rotated")
        v_hi_made = sem("v_hi_made")
        rstd_x1, rstd_mix, rstd_ff = sem("rstd_x1"), sem("rstd_mix"), sem("rstd_ff")
        s_done, s_masked, m_made, p_exp, p_normed = (sem(n) for n in ("s_done", "s_masked", "m_made", "p_exp", "p_normed"))
        pT_done, pT_hi_made, pT_lo_made = sem("pT_done"), sem("pT_hi_made"), sem("pT_lo_made")
        pT_masked = sem("pT_masked")
        o_done, o_part_made, o_sum_made = sem("o_done"), sem("o_part_made"), sem("o_sum_made")
        o_hi_made, o_lo_made = sem("o_hi_made"), sem("o_lo_made")
        sig_made, u_made, ln_summed = sem("sig_made"), sem("u_made"), sem("ln_summed")
        ws_turned, ws_copied = sem("ws_turned"), sem("ws_copied")
        ln_var, v_normed = sem("ln_var"), sem("v_normed")
        mix_done, a_made, a_hi, a_lo = sem("mix_done"), sem("a_made"), sem("a_hi"), sem("a_lo")
        merged, merged_hi, merged_lo = sem("merged"), sem("merged_hi"), sem("merged_lo")
        x1_made = sem("x1_made")
        sq_made, ff_hi_made, ff_lo_made = sem("sq_made"), sem("ff_hi_made"), sem("ff_lo_made")
        y_made = sem("y_made")
        dve_step, act_step, pool_step = sem("dve_step"), sem("act_step"), sem("pool_step")

        q_pair = (actA_hi, actA_lo)

        block = ctx.enter_context(nc.Block())

        def stationary(ring, j):
            return ring[:, j].rearrange("p (k n) -> p k n", k=KT)

        def moving(ring, j):
            return ring[:, j].rearrange("p (k n) -> p k n", n=COL)

        @block.sync
        def _(sp):
            def slot_free(u):
                sp.wait_ge(lo_made, u - SLOTS + 1)

            def load_columns(j, w, col):
                sp.dma_start(stationary(w_raw, j), w[:, 0:KT, col]).then_inc(w_loaded[j], 16)

            def load_rows(j, w, k, col):
                sp.dma_start(moving(w_raw, j), w[:, k:k + 2, col]).then_inc(w_loaded[j], 16)

            def load_x(t):
                sp.dma_start(x0[:, t], x_v[:, t]).then_inc(x_in[t], 16)

            load_x(0)
            load_x(1)
            sp.dma_start(g_pre[:], norm_mix_pre[0:1, :].to_broadcast([P, D])).then_inc(g_pre_in, 16)
            for j in (0, 1):
                load_rows(j, w_in_v, 2 * j, slice(C_Q, C_Q + COL))
            load_x(2)
            load_x(3)
            for j in (2, 3):
                load_rows(j, w_in_v, 2 * j, slice(C_Q, C_Q + COL))
            with sp.Fori(1, 3) as b:
                for j in range(SLOTS):
                    slot_free(b * SLOTS + j)
                    load_rows(j, w_in_v, 2 * j, bass.ds(b * COL + C_Q, COL))
            with sp.Fori(0, 4) as i:
                for j in range(SLOTS):
                    slot_free(i * SLOTS + (U_SIDE + j))
                    load_columns(j, w_in_v, bass.ds(i * (SLOTS * P) + (C_GATES + j * P), P))
            with sp.Fori(0, 2) as i:
                for j in range(SLOTS):
                    slot_free(i * SLOTS + (U_SIDE + 2 * KT + j))
                    load_columns(j, w_in_v, bass.ds(i * (SLOTS * P) + (C_U + j * P), P))
            with sp.Fori(0, 2) as b:
                for j in range(SLOTS):
                    slot_free(b * SLOTS + (U_VSGU + j))
                    load_rows(j, w_in_v, 2 * j, bass.ds(b * COL + C_V, COL))
            sp.wait_ge(o_lo_made, STEPS)
            sp.dma_start(w_s[:], w_spatial[0].rearrange("g t s -> t g s")).then_inc(ws_in, 16)
            sp.dma_start(ln_g[:], ln_v_gain[0:1, :].to_broadcast([P, D])).then_inc(sgu_in, 16)
            sp.dma_start(ln_b[:], ln_v_bias[0:1, :].to_broadcast([P, D])).then_inc(sgu_in, 16)
            sp.dma_start(b_s[:], b_spatial[0:1].to_broadcast([P, GROUPS, P])).then_inc(sgu_in, 16)
            with sp.Fori(0, 2) as i:
                for j in range(SLOTS):
                    slot_free(i * SLOTS + (U_WB + j))
                    load_columns(j, w_b_v, bass.ds(i * (SLOTS * P) + j * P, P))
            with sp.Fori(0, 2) as i:
                for j in range(SLOTS):
                    slot_free(i * SLOTS + (U_WA + j))
                    load_columns(j, w_a_v, bass.ds(i * (SLOTS * P) + j * P, P))
            sp.wait_ge(a_made, GROUPS)
            sp.dma_start(x1[:], x_v[:, :, :]).then_inc(x_again, 16)
            sp.dma_start(g_mix_post[:], norm_mix_post[0:1, :].to_broadcast([P, D])).then_inc(wo_in, 16)
            sp.dma_start(g_ff_pre[:], norm_ff_pre[0:1, :].to_broadcast([P, D])).then_inc(wo_in, 16)
            with sp.Fori(0, 2) as b:
                for j in range(SLOTS):
                    slot_free(b * SLOTS + (U_WO + j))
                    load_rows(j, w_o_v, 2 * j, bass.ds(b * COL, COL))
            for c in range(2):
                first = U_FF + c * U_HALF
                with sp.Fori(0, HALF_K // SLOTS) as i:
                    for j in range(SLOTS):
                        slot_free(i * SLOTS + (first + j))
                        load_columns(j, w_ff_in_v, bass.ds(i * (SLOTS * P) + (c * HALF_K + j) * P, P))
                if c == 0:
                    sp.wait_ge(pe_done, UNIT_DONE[U_FF - 1])
                    sp.dma_start(g_ff_post[:], norm_ff_post[0:1, :].to_broadcast([P, D])).then_inc(g_ff_in, 16)
                with sp.Fori(0, 2) as h:
                    for n in range(HALF_K // 2):
                        slot_free(h * (HALF_K // 2) + (first + HALF_K + n))
                        load_rows(n % SLOTS, w_ff_out_v, c * HALF_K + 2 * n, bass.ds(h * COL, COL))
            for t in range(TT):
                for h in range(2):
                    cols = slice(h * COL, (h + 1) * COL)
                    sp.wait_ge(y_made, 2 * t + h + 1)
                    sp.dma_start(out_v[:, t, cols], ff_sum[:, t, cols]).then_inc(stored, 16)
            sp.wait_ge(stored, 2 * 16 * TT)

        @block.gpsimd
        def _(pool):
            steps = [0]

            def after(ins):
                steps[0] += 1
                ins.then_inc(pool_step, 1)
                pool.wait_ge(pool_step, steps[0])

            after(nc.gpsimd.memset(neg_half[:], -0.5))
            after(nc.gpsimd.memset(ident[:], 0.0))
            nc.gpsimd.affine_select(out=ident[:], in_=ident[:], compare_op=ALU.not_equal, fill=1.0, base=0,
                                    pattern=[[-1, P]], channel_multiplier=1).then_inc(pool_consts, 1)

            def power(norm, t, signal):
                nc.gpsimd.tensor_tensor(rstd[:, norm, t:t + 1], var_eps[:, norm, t:t + 1], neg_half[:],
                                        ALU.pow).then_inc(signal, 1)

            def inv_sqrt(mean, norm, t, signal):
                after(nc.gpsimd.tensor_scalar(var_eps[:, norm, t:t + 1], mean, EPS, None, ALU.add))
                power(norm, t, signal)

            for t in range(TT):
                pool.wait_ge(ssq_act if t else ssq_dve, max(t, 1))
                inv_sqrt(ssq[:, 0, t:t + 1], 0, t, rstd_made)
            for i in range(ROT):
                last = nc.gpsimd.memset(inv_freq[:, i:i + 1], INV_FREQ[i])
            last.then_inc(pool_consts, 1)
            after(nc.gpsimd.memset(mask[:], 0.0))
            after(nc.gpsimd.affine_select(out=mask[:], in_=mask[:], compare_op=ALU.is_gt, fill=NEG, base=0,
                                          pattern=[[1, 2 * P]], channel_multiplier=-1))
            nc.gpsimd.affine_select(out=mask[:], in_=mask[:], compare_op=ALU.is_ge, fill=NEG, base=P,
                                    pattern=[[-1, 2 * P]], channel_multiplier=1).then_inc(pool_consts, 1)
            def part(pT, block):
                pattern, sign, op = ([[0, QPK], [-1, P]], 1, ALU.is_gt) if block == 0 else (
                    [[0, QPK], [1, P]], -1, ALU.is_ge)
                return nc.gpsimd.affine_select(out=pT[:, block].rearrange("p (h q) -> p h q", q=P),
                                               in_=pT[:, 1].rearrange("p (h q) -> p h q", q=P), compare_op=op,
                                               fill=0.0, base=0, pattern=pattern, channel_multiplier=sign)

            for s in range(NKV, STEPS):
                pool.wait_ge(pT_hi_made, s + 1)
                after(part(pT_hi, 0))
                pool.wait_ge(pT_lo_made, s + 1)
                part(pT_hi, 1)
                part(pT_lo, 0).then_inc(pT_masked, 1)
                pool.wait_ge(pT_masked, 2 * (s - NKV) + 1)
                part(pT_lo, 1).then_inc(pT_masked, 1)
            pool.wait_ge(ws_copied, 2)
            nc.gpsimd.affine_select(out=w_mix[:], in_=w_mix[:], compare_op=ALU.is_ge, fill=0.0, base=0,
                                    pattern=[[0, GROUPS], [1, P]], channel_multiplier=-1).then_inc(w_mix_made, 1)
            for t in range(TT):
                pool.wait_ge(ln_var, t + 1)
                inv_sqrt(ln_mv[:, t, 1:2], 1, t, rstd_made)

            def halves(part, norm, t, signal):
                after(nc.gpsimd.tensor_tensor(var_eps[:, norm, t:t + 1], ssq_eps[:, part // 4, t:t + 1],
                                              ssq[:, part + 1, t:t + 1], ALU.add))
                power(norm, t, signal)

            def first_half(part, counted):
                pool.wait_ge(ssq_act, counted)
                after(nc.gpsimd.tensor_scalar(ssq_eps[:, part // 4], ssq[:, part], EPS, None, ALU.add))

            first_half(1, Q_MIX + TT)
            for kind, t in WO_ORDER["pool"]:
                if kind == "mix":
                    pool.wait_ge(ssq_act, Q_MIX + TT + t + 1)
                    halves(1, 2, t, rstd_mix)
                else:
                    pool.wait_ge(ssq_x1, t + 1)
                    inv_sqrt(ssq[:, 3, t:t + 1], 3, t, rstd_x1)
            pool.wait_ge(pe_done, UNIT_DONE[U_FF - 1])
            nc.gpsimd.memset(ff_sum[:], 0.0).then_inc(ff_zeroed, 1)
            first_half(4, Q_MIX + 3 * TT)
            for t in range(TT):
                pool.wait_ge(ssq_act, Q_MIX + 3 * TT + t + 1)
                halves(4, 4, t, rstd_ff)

        @block.scalar
        def _(act):
            def round_unit(j, loads, used):
                act.wait_ge(w_loaded[j], loads)
                if used is not None:
                    act.wait_ge(pe_done, used)
                nc.scalar.activation(w_hi[:, j], w_raw[:, j], ACT.Copy).then_inc(hi_made, 1)

            def hi_of(u):
                round_unit(u % SLOTS, 16 * (u // SLOTS + 1), UNIT_DONE[u - SLOTS] if u >= SLOTS else None)

            def hi_after(i, u, per=SLOTS):
                counts = UNIT_DONE[u + per] - UNIT_DONE[u]
                round_unit(u % SLOTS, i * (16 * per // SLOTS) + 16 * (u // SLOTS + 2), i * counts + UNIT_DONE[u])

            act.dma_start(pos_i[:], pos_v, allow_slow_non_contiguous=True).then_inc(consts_in, 16)
            act.dma_start(sink_b[:], sinks[0:1, :].to_broadcast([P, NQ])).then_inc(consts_in, 16)

            def turned_tile(t):
                p = 2 * (t % 2)
                return aux[:, p:p + 2].rearrange("p a (k s) -> p (a k) s", s=P)

            def turn_hi(base, t, hi):
                act.wait_ge(turned, base + t + 1)
                nc.scalar.activation(hi[:, :, t * P:(t + 1) * P], turned_tile(t), ACT.Copy).then_inc(turned_hi, 1)

            def square(t):
                act.wait_ge(x_in[t], 16)
                if t > 1:
                    act.wait_ge(ssq_act, t - 1)
                nc.scalar.activation(probs[:].rearrange("p h k -> p (h k)"), x0[:, t], ACT.Square, scale=ROOT_MEAN,
                                     accum_out=ssq[:, 0, t:t + 1]).then_inc(ssq_act, 1)

            square(1)
            hi_of(0)
            turn_hi(0, 0, actB_hi)
            turn_hi(0, 1, actB_hi)
            hi_of(1)
            square(2)
            square(3)
            turn_hi(0, 2, actB_hi)
            turn_hi(0, 3, actB_hi)
            hi_of(2)
            hi_of(3)
            act.wait_ge(angles, 2)
            nc.scalar.activation(sin_t[:], sin_arg[:], ACT.Sin).then_inc(sincos, 1)
            nc.scalar.activation(cos_t[:], cos_arg[:], ACT.Sin).then_inc(sincos, 1)

            def q_out(b, t):
                act.wait_ge(pe_done, BANK_DONE[(b + 1) * SLOTS - 1, t])
                nc.scalar.activation(qk[:, t, b * 8:(b + 1) * 8, :], acc[:, t].rearrange("p (h d) -> p h d", d=HD),
                                     ACT.Copy, scale=HD ** -0.5).then_inc(acc_to_act, 1)

            for b in range(2):
                for j in range(SLOTS):
                    if j == SLOTS - 1:
                        for t in range(TT):
                            q_out(b, t)
                    hi_of((b + 1) * SLOTS + j)
            for j in range(SLOTS):
                if j == SLOTS - 1:
                    for t in range(TT):
                        act.wait_ge(pe_done, BANK_DONE[U_SIDE - 1, t])
                        kv = acc[:, t].rearrange("p (c g d) -> p c g d", c=2, d=HD)
                        nc.scalar.activation(qk[:, t, NQ:NH].rearrange("p (g r) d -> p g r d", r=2),
                                             kv[:, 0].unsqueeze(2).to_broadcast([P, NKV, 2, HD]), ACT.Copy)
                        nc.scalar.activation(v_pair[:, t, :, 0:HD], kv[:, 1], ACT.Copy).then_inc(v_hi_made, 1)
                hi_of(2 * SLOTS + j + SLOTS)

            def side_out(n):
                act.wait_ge(pe_done, UNIT_DONE[U_SIDE + n])
                dst = gates[:, n] if n < 2 * KT else u_sb[:, n - 2 * KT]
                nc.scalar.activation(dst, acc[:, n % 2], ACT.Copy).then_inc(acc_to_act, 1)
                hi_of(U_SIDE + n + SLOTS)

            for n in range(SIDE_AHEAD):
                side_out(n)
                for k in range(3 * n, 3 * n + 3):
                    act.wait_ge(turned, T_QK + k + 1)
                    if k < KT:
                        for f in range(2):
                            last = nc.scalar.activation(q_pair[f][0:HD, k], aux[HD * f:HD * (f + 1), k % 4], ACT.Copy)
                    else:
                        last = nc.scalar.activation(kT_hi[:, k - KT], aux[:, k % 4], ACT.Copy)
                    last.then_inc(turned_hi, 1)

            for slot in range(SLOT_COUNT):
                for n in side_finished(slot):
                    side_out(n)
                if slot >= 2:
                    s = slot - 2
                    act.wait_ge(o_done, s + 1)
                    if s >= 2:
                        act.wait_ge(o_sum_made, s - 1)
                    for f in range(2):
                        src = acc[HD * (1 - f):HD * (2 - f), 2 + s % 2, 2 * P * f:2 * P * (f + 1)]
                        last = nc.scalar.activation(o_part[HD * f:HD * (f + 1), s % 2],
                                                    src.rearrange("p (m q) -> p m q", m=2), ACT.Copy)
                    last.then_inc(o_part_made, 1)
                if 1 <= slot <= STEPS:
                    s = slot - 1
                    act.wait_ge(pT_done, s + 1)
                    nc.scalar.activation(pT_hi[:, 1], aux[:, 2 + s % 2], ACT.Copy).then_inc(pT_hi_made, 1)
                if slot < STEPS:
                    s = slot
                    off = P if s < NKV else 0
                    act.wait_ge(m_made, s + 1)
                    for h in range(QPK):
                        nc.scalar.activation(probs[:, h, off:], scores_sb[:, h, off:], ACT.Exp,
                                             bias=neg_m[:, h:h + 1], accum_out=denom[:, h:h + 1])
                    nc.scalar.activation(sink_e[:], sink_m[:], ACT.Exp).then_inc(p_exp, 1)
                if slot >= 2:
                    s = slot - 2
                    b, g = divmod(s, NKV)
                    act.wait_ge(o_sum_made, s + 1)
                    nc.scalar.activation(actA_hi[:, 2 * g:2 * g + 2, P * b:P * b + P], o_sum[:, s % 2],
                                         ACT.Copy).then_inc(o_hi_made, 1)

            act.wait_ge(acc_to_act, A_VSGU)
            for b in range(2):
                for j in range(SLOTS - 1):
                    if b == 0:
                        for q in ((2,), (3,), (0, 1))[j]:
                            part = gates[:, 4 * q:4 * q + 4]
                            nc.scalar.activation(part, part, ACT.Sigmoid).then_inc(sig_made, 1)
                        hi_of(U_VSGU + SLOTS + j)
                    else:
                        hi_of(U_WB + j)
                        if j == 0:
                            for h in range(2):
                                act.wait_ge(ws_turned, h + 1)
                                nc.scalar.activation(w_mix[:, 4 * h:4 * h + 4],
                                                     aux[:, h].rearrange("p (g t) -> p g t", g=4),
                                                     ACT.Copy).then_inc(ws_copied, 1)
                        else:
                            part = u_sb[:, 4 * (j - 1):4 * j]
                            nc.scalar.activation(part, part, ACT.Gelu_apprx_tanh).then_inc(u_made, 1)
                for t in range(TT):
                    act.wait_ge(pe_done, BANK_DONE[U_VSGU + (b + 1) * SLOTS - 1, t])
                    nc.scalar.activation(v_sgu[:, t, b * COL:(b + 1) * COL], acc[:, t],
                                         ACT.Gelu_apprx_tanh).then_inc(acc_to_act, 1)
                hi_of(U_VSGU + (b + 2) * SLOTS - 1)
            for n in range(KT):
                hi_of(U_WB + n + SLOTS)
                for g in mix_groups_after(n):
                    act.wait_ge(a_made, g + 1)
                    nc.scalar.activation(actB_hi[:, g], u_sb[:, g], ACT.Copy).then_inc(a_hi, 1)
            with act.Fori(0, 2) as i:
                for j in range(SLOTS):
                    act.wait_ge(merged, i * SLOTS + (j + 1))
                    nc.scalar.activation(actA_hi[:, bass.ds(i * SLOTS + j, 1)].rearrange("p k s -> p (k s)"),
                                         gates[:, bass.ds(i * SLOTS + j, 1)].rearrange("p k s -> p (k s)"),
                                         ACT.Copy).then_inc(merged_hi, 1)
                    hi_after(i, U_WA + j)

            for j in range(SLOTS):
                if j == SLOTS - 1:
                    for t in range(TT):
                        act.wait_ge(pe_done, BANK_DONE[U_WO + SLOTS - 1, t])
                        nc.scalar.activation(mix[:, t, 0:COL], acc[:, t], ACT.Copy).then_inc(acc_to_act, 1)
                hi_of(U_WO + SLOTS + j)

            def mix_square(part, t, src, signal):
                if part:
                    act.wait_ge(*part)
                nc.scalar.activation(junk_wo[:, 0:src.shape[1]], src, ACT.Square, scale=ROOT_MEAN,
                                     accum_out=ssq[:, t[0], t[1]:t[1] + 1]).then_inc(signal, 1)

            act.wait_ge(wo_in, 32)
            for t in range(TT):
                act.wait_ge(acc_to_act, A_WO + t + 1)
                mix_square((ssq_act, Q_MIX + t), (1, t), mix[:, t, 0:COL], ssq_act)
            for kind, t in WO_ORDER["act"]:
                if kind == "sq":
                    act.wait_ge(pe_done, BANK_DONE[U_FF - 1, t])
                    if t:
                        act.wait_ge(ssq_x1, min(t, SQX_BEFORE[t]))
                    mix_square((ssq_act, Q_MIX + TT + t), (2, t), acc[:, t], ssq_act)
                elif kind == "sqx":
                    act.wait_ge(x1_made, t + 1)
                    act.wait_ge(ssq_act, Q_MIX + TT + SQ_BEFORE[t])
                    mix_square((ssq_x1, t) if t else None, (3, t), x1[:, t], ssq_x1)
                elif kind == "turn":
                    turn_hi(T_FF, t, actB_hi)
                else:
                    hi_of(U_FF + t)

            for c in range(2):
                first = U_FF + c * U_HALF
                with act.Fori(0, HALF_K // SLOTS) as i:
                    for j in range(SLOTS):
                        act.wait_ge(pe_done, i * SLOTS + UNIT_DONE[first + j])
                        nc.scalar.activation(relu_b[:, j % 2], acc[:, j], ACT.Relu).then_inc(acc_to_act, 1)
                        hi_after(i, first + j)
                        act.wait_ge(sq_made, i * SLOTS + (c * HALF_K + j + 1))
                        nc.scalar.activation(ff_hi[:, bass.ds(i * SLOTS + j, 1)].rearrange("p k s -> p (k s)"),
                                             sq_b[:, j % 2], ACT.Copy).then_inc(ff_hi_made, 1)
                if c == 0:
                    with act.Fori(0, 2) as h:
                        for n in range(HALF_K // 2):
                            hi_after(h, first + HALF_K + n, HALF_K // 2)
                else:
                    for n in range(HALF_K // 2):
                        hi_of(first + HALF_K + SLOTS + n)
                    for h in range(2):
                        for t in range(TT):
                            act.wait_ge(acc_to_dve, V_FF + (2 + h) * TT + t + 1)
                            act.wait_ge(ssq_act, Q_MIX + (2 + h) * TT + t)
                            nc.scalar.activation(junk_ff[:, 0:COL], ff_sum[:, t, h * COL:(h + 1) * COL], ACT.Square,
                                                 scale=ROOT_MEAN, accum_out=ssq[:, 4 + h, t:t + 1]
                                                 ).then_inc(ssq_act, 1)
                        if h == 0:
                            for j in range(SLOTS):
                                hi_of(UNITS - SLOTS + j)

        @block.vector
        def _(dve):
            steps = [0]

            def after(ins):
                steps[0] += 1
                ins.then_inc(dve_step, 1)
                dve.wait_ge(dve_step, steps[0])

            def lo_of(u, j):
                dve.wait_ge(hi_made, u + 1)
                nc.vector.tensor_tensor(w_lo[:, j], w_raw[:, j], w_hi[:, j].bitcast(F32),
                                        ALU.subtract).then_inc(lo_made, 1)

            def turned_tile(t):
                p = 2 * (t % 2)
                return aux[:, p:p + 2].rearrange("p a (k s) -> p (a k) s", s=P)

            def turn_lo(base, t, hi, lo):
                dve.wait_ge(turned_hi, base + t + 1)
                at = (slice(None), slice(None), slice(t * P, (t + 1) * P))
                nc.vector.tensor_tensor(lo[at], turned_tile(t), hi[at].bitcast(F32), ALU.subtract).then_inc(turned_lo, 1)

            dve.wait_ge(x_in[0], 16)
            nc.vector.tensor_tensor_reduce(scores_sb[:].rearrange("p h k -> p (h k)"), x0[:, 0], x0[:, 0],
                                           1.0 / D, 0.0, ALU.mult, ALU.add, ssq[:, 0, 0:1]).then_inc(ssq_dve, 1)

            def norm(t):
                dve.wait_ge(rstd_made, t + 1)
                nc.vector.scalar_tensor_tensor(x0[:, t], x0[:, t], rstd[:, 0, t:t + 1], g_pre[:], ALU.mult,
                                               ALU.mult).then_inc(normed, 1)

            dve.wait_ge(g_pre_in, 16)
            norm(0)
            norm(1)
            lo_of(0, 0)
            turn_lo(0, 0, actB_hi, actB_lo)
            turn_lo(0, 1, actB_hi, actB_lo)
            lo_of(1, 1)
            norm(2)
            norm(3)
            turn_lo(0, 2, actB_hi, actB_lo)
            turn_lo(0, 3, actB_hi, actB_lo)
            lo_of(2, 2)
            lo_of(3, 3)

            def stt(o, a, s, b, op0=ALU.mult, op1=ALU.add):
                after(nc.vector.scalar_tensor_tensor(o, a, s, b, op0, op1))

            def ts(o, a, s1, s2, op0, op1=ALU.bypass):
                if s2 is None:
                    after(nc.vector.tensor_scalar(o, a, s1, None, op0))
                else:
                    after(nc.vector.tensor_scalar(o, a, s1, s2, op0, op1))

            dve.wait_ge(pool_consts, 2)
            dve.wait_ge(consts_in, 32)
            after(nc.vector.tensor_copy(pos_f[:], pos_i[:]))
            after(nc.vector.tensor_tensor(ang[:], pos_f[:].unsqueeze(2).to_broadcast([P, TT, ROT]),
                                          inv_freq[:].unsqueeze(1).to_broadcast([P, TT, ROT]), ALU.mult))
            ts(turns[:], ang[:], 1.0 / (2 * np.pi), ROUND, ALU.mult, ALU.add)
            ts(turns[:], turns[:], -ROUND, None, ALU.add)
            ts(turns_hi[:], turns[:], 2.0 ** -12, ROUND, ALU.mult, ALU.add)
            ts(turns_hi[:], turns_hi[:], -ROUND, 2.0 ** 12, ALU.add, ALU.mult)
            after(nc.vector.tensor_tensor(turns[:], turns[:], turns_hi[:], ALU.subtract))
            for part in TWO_PI:
                stt(ang[:], turns_hi[:], -part, ang[:])
                stt(ang[:], turns[:], -part, ang[:])
            for arg, shift in ((sin_arg, 0.0), (cos_arg, np.pi / 2)):
                ts(arg[:], ang[:], float(shift), None, ALU.add)
                ts(turns[:], arg[:], 1.0 / (2 * np.pi), ROUND, ALU.mult, ALU.add)
                ts(turns[:], turns[:], -ROUND, None, ALU.add)
                stt(arg[:], turns[:], -float(np.float32(2 * np.pi)), arg[:])
                stt(arg[:], turns[:], float(np.float32(2 * np.pi)) - 2 * np.pi, arg[:])
                nc.vector.tensor_scalar(arg[:], arg[:], -PI32, PI32, ALU.max, ALU.min).then_inc(angles, 1)
            after(nc.vector.tensor_scalar(neg_sink[:], sink_b[:], -1.0, None, ALU.mult))

            with dve.Fori(0, 2) as b:
                for j in range(SLOTS):
                    lo_of(b * SLOTS + (SLOTS + j), j)

            def rotate(h0, h1):
                n = h1 - h0
                r1, r2 = qk[:, :, h0:h1, 0:ROT], qk[:, :, h0:h1, ROT:2 * ROT]
                c = cos_t[:].unsqueeze(2).to_broadcast([P, TT, n, ROT])
                s = sin_t[:].unsqueeze(2).to_broadcast([P, TT, n, ROT])
                x1c, x2s, x2c, x1s = (r[:, :, 0:n] for r in rot)
                if h0:
                    dve.wait_ge(rotated, 1)
                nc.vector.tensor_tensor(x1c, r1, c, ALU.mult)
                nc.vector.tensor_tensor(x2s, r2, s, ALU.mult)
                nc.vector.tensor_tensor(x2c, r2, c, ALU.mult)
                after(nc.vector.tensor_tensor(x1s, r1, s, ALU.mult))
                nc.vector.tensor_tensor(r1, x1c, x2s, ALU.subtract)
                nc.vector.tensor_tensor(r2, x2c, x1s, ALU.add).then_inc(rotated, 1)

            lo_of(3 * SLOTS, 0)
            dve.wait_ge(sincos, 2)
            dve.wait_ge(acc_to_act, A_SIDE)
            rotate(0, NQ)
            lo_of(3 * SLOTS + 1, 1)
            lo_of(3 * SLOTS + 2, 2)
            for t in range(TT):
                dve.wait_ge(v_hi_made, t + 1)
                nc.vector.tensor_tensor(v_pair[:, t, :, HD:2 * HD],
                                        acc[:, t, 2 * P:4 * P].rearrange("p (g d) -> p g d", d=HD),
                                        v_pair[:, t, :, 0:HD].bitcast(F32), ALU.subtract).then_inc(acc_to_dve, 1)
            rotate(NQ, NH)
            lo_of(3 * SLOTS + 3, 3)

            for n in range(SIDE_AHEAD):
                for k in range(3 * n, 3 * n + 3):
                    dve.wait_ge(turned_hi, T_QK + k + 1)
                    if k < KT:
                        for f in range(2):
                            last = nc.vector.tensor_tensor(q_pair[f][HD:P, k], aux[HD * f:HD * (f + 1), k % 4],
                                                           q_pair[f][0:HD, k].bitcast(F32), ALU.subtract)
                    else:
                        last = nc.vector.tensor_tensor(kT_lo[:, k - KT], aux[:, k % 4], kT_hi[:, k - KT].bitcast(F32),
                                                       ALU.subtract)
                    last.then_inc(turned_lo, 1)
                lo_of(U_SIDE + n + SLOTS, n)

            dve.wait_ge(pool_consts, 3)
            for slot in range(SLOT_COUNT):
                for n in side_finished(slot):
                    lo_of(U_SIDE + n + SLOTS, n % SLOTS)
                if slot >= 2:
                    s = slot - 2
                    dve.wait_ge(o_part_made, s + 1)
                    if s >= 2:
                        dve.wait_ge(o_lo_made, s - 1)
                        dve.wait_ge(o_hi_made, s - 1)
                    for f in range(2):
                        half = slice(HD * f, HD * (f + 1))
                        src = acc[half, 2 + s % 2, 2 * P * f:2 * P * (f + 1)].rearrange("p (m q) -> p m q", m=2)
                        last = nc.vector.tensor_tensor(o_sum[half, s % 2], src, o_part[half, s % 2], ALU.add)
                    last.then_inc(o_sum_made, 1)
                if slot < STEPS:
                    s = slot
                    g = s % NKV
                    off = P if s < NKV else 0
                    dve.wait_ge(s_done, s + 1)
                    for h in range(QPK):
                        f, m = divmod(h, 2)
                        last = nc.vector.tensor_tensor_reduce(
                            scores_sb[:, h, off:], aux[:, f, 2 * P * m + off:2 * P * (m + 1)], mask[:, off:],
                            1.0, -3e38, ALU.add, ALU.max, row_max[:, h:h + 1])
                    last.then_inc(s_masked, 1)
                    dve.wait_ge(s_masked, s + 1)
                    heads = slice(QPK * g, QPK * (g + 1))
                    by_half = lambda a: a[:, heads].rearrange("p (m f) -> p f m", f=2)
                    v2 = lambda a: a[:].rearrange("p (f m) -> p f m", f=2)
                    after(nc.vector.scalar_tensor_tensor(v2(neg_m), v2(row_max), -1.0, by_half(neg_sink),
                                                         ALU.mult, ALU.min))
                    nc.vector.tensor_tensor(v2(sink_m), by_half(sink_b), v2(neg_m), ALU.add).then_inc(m_made, 1)
                if 1 <= slot <= STEPS:
                    s = slot - 1
                    dve.wait_ge(pT_hi_made, s + 1)
                    nc.vector.tensor_tensor(pT_lo[:, 1], aux[:, 2 + s % 2], pT_hi[:, 1].bitcast(F32),
                                            ALU.subtract).then_inc(pT_lo_made, 1)
                if slot < STEPS:
                    s = slot
                    dve.wait_ge(p_exp, s + 1)
                    own = probs[:, :, P:2 * P]
                    if off == 0:
                        nc.vector.tensor_tensor(own, probs[:, :, 0:P], own, ALU.add)
                    after(nc.vector.tensor_tensor(denom2[:], denom[:], sink_e[:], ALU.add))
                    after(nc.vector.reciprocal(r_denom[:], denom2[:]))
                    for h in range(QPK):
                        last = nc.vector.tensor_scalar(own[:, h], own[:, h], r_denom[:, h:h + 1],
                                                       None, ALU.mult)
                    last.then_inc(p_normed, 1)
                if slot >= 2:
                    s = slot - 2
                    b, g = divmod(s, NKV)
                    at = (slice(None), slice(2 * g, 2 * g + 2), slice(P * b, P * b + P))
                    dve.wait_ge(o_hi_made, s + 1)
                    dve.wait_ge(o_sum_made, s + 1)
                    nc.vector.tensor_tensor(actA_lo[at], o_sum[:, s % 2], actA_hi[at].bitcast(F32),
                                            ALU.subtract).then_inc(o_lo_made, 1)

            for b in range(2):
                for j in range(SLOTS):
                    lo_of(U_VSGU + (b + 1) * SLOTS + j, j)
                for t in range(TT):
                    dve.wait_ge(acc_to_act, A_VSGU + b * TT + t + 1)
                    nc.vector.bn_stats(ln_stats[:, t, b], v_sgu[:, t, b * COL:(b + 1) * COL]).then_inc(ln_summed, 1)
            dve.wait_ge(ln_summed, 2 * TT)
            for t in range(TT):
                nc.vector.bn_aggr(ln_mv[:, t], ln_stats[:, t]).then_inc(ln_var, 1)
            dve.wait_ge(sgu_in, 48)

            def layer_norm(t):
                dve.wait_ge(ln_var, t + 1)
                after(nc.vector.scalar_tensor_tensor(v_sgu[:, t], v_sgu[:, t], ln_mv[:, t, 0:1], ln_g[:],
                                                     ALU.subtract, ALU.mult))
                dve.wait_ge(rstd_made, TT + t + 1)
                nc.vector.scalar_tensor_tensor(v_sgu[:, t], v_sgu[:, t], rstd[:, 1, t:t + 1], ln_b[:],
                                               ALU.mult, ALU.add).then_inc(v_normed, 1)

            for n in range(KT):
                if n < 2:
                    layer_norm(2 * n)
                    layer_norm(2 * n + 1)
                own = gates[:, KT + n]
                dve.wait_ge(sig_made, n // SLOTS + 1)
                dve.wait_ge(pe_done, UNIT_DONE[U_WB + n])
                nc.vector.tensor_tensor(own, acc[:, n % 4], own, ALU.mult).then_inc(acc_to_dve, 1)
                lo_of(U_WB + n + SLOTS, n % SLOTS)
                for g in mix_groups_after(n):
                    bias = b_s[:, g].unsqueeze(1).to_broadcast([P, TT, P])
                    mixed = aux[:, g % 4].rearrange("p (c t) -> p c t", t=P)
                    tmp = w_s[:, TT * (g % 2):TT * (g % 2 + 1)]
                    dve.wait_ge(mix_done, g + 1)
                    after(nc.vector.tensor_tensor(tmp, mixed, bias, ALU.add))
                    dve.wait_ge(u_made, g // 4 + 1)
                    u_g = u_sb[:, g].rearrange("p (c t) -> p c t", t=P)
                    nc.vector.tensor_tensor(u_g, u_g, tmp, ALU.mult).then_inc(a_made, 1)
                    dve.wait_ge(a_hi, g + 1)
                    nc.vector.tensor_tensor(actB_lo[:, g], u_sb[:, g], actB_hi[:, g].bitcast(F32),
                                            ALU.subtract).then_inc(a_lo, 1)
            dve.wait_ge(sig_made, 4)
            with dve.Fori(0, 2) as i:
                for j in range(SLOTS):
                    at = lambda k0: gates[:, bass.ds(i * SLOTS + (k0 + j), 1)].rearrange("p k s -> p (k s)")
                    dve.wait_ge(pe_done, i * SLOTS + UNIT_DONE[U_WA + j])
                    nc.vector.tensor_tensor(at(0), acc[:, j], at(0), ALU.mult).then_inc(acc_to_dve, 1)
                    dve.wait_ge(acc_to_dve, i * SLOTS + (V_WA + j + 1))
                    nc.vector.tensor_tensor(at(0), at(0), at(KT), ALU.add).then_inc(merged, 1)
                    dve.wait_ge(merged_hi, i * SLOTS + (j + 1))
                    dst = bass.ds(i * SLOTS + j, 1)
                    nc.vector.tensor_tensor(actA_lo[:, dst].rearrange("p k s -> p (k s)"), at(0),
                                            actA_hi[:, dst].rearrange("p k s -> p (k s)").bitcast(F32),
                                            ALU.subtract).then_inc(merged_lo, 1)
                    lo_of(i * SLOTS + (U_WA + SLOTS + j), j)
            for j in range(SLOTS):
                lo_of(U_WO + SLOTS + j, j)
            dve.wait_ge(wo_in, 32)
            dve.wait_ge(x_again, 16)
            for t in range(TT):
                dve.wait_ge(ssq_act, Q_MIX + t + 1)
                last = nc.vector.tensor_tensor(mix[:, t, 0:COL], mix[:, t, 0:COL], g_mix_post[:, 0:COL], ALU.mult)
            last.then_inc(half_scaled, 1)
            for kind, t in WO_ORDER["dve"]:
                if kind == "mix":
                    dve.wait_ge(ssq_act, Q_MIX + TT + t + 1)
                    nc.vector.tensor_tensor(mix[:, t, COL:D], acc[:, t], g_mix_post[:, COL:D],
                                            ALU.mult).then_inc(acc_to_dve, 1)
                elif kind == "x1":
                    dve.wait_ge(rstd_mix, t + 1)
                    dve.wait_ge(acc_to_dve, V_WO + t + 1)
                    if t == 0:
                        dve.wait_ge(half_scaled, 1)
                    nc.vector.scalar_tensor_tensor(x1[:, t], mix[:, t], rstd[:, 2, t:t + 1], x1[:, t], ALU.mult,
                                                   ALU.add).then_inc(x1_made, 1)
                elif kind == "norm":
                    dve.wait_ge(rstd_x1, t + 1)
                    dve.wait_ge(x1_made, t + 1)
                    nc.vector.scalar_tensor_tensor(mix[:, t], x1[:, t], rstd[:, 3, t:t + 1], g_ff_pre[:], ALU.mult,
                                                   ALU.mult).then_inc(normed, 1)
                elif kind == "turn":
                    turn_lo(T_FF, t, actB_hi, actB_lo)
                else:
                    lo_of(U_FF + t, t)
            for c in range(2):
                first = U_FF + c * U_HALF
                relus = A_FF + c * HALF_K
                with dve.Fori(0, HALF_K // SLOTS) as i:
                    for j in range(SLOTS):
                        dve.wait_ge(acc_to_act, i * SLOTS + (relus + j + 1))
                        nc.vector.tensor_tensor(sq_b[:, j % 2], relu_b[:, j % 2], relu_b[:, j % 2],
                                                ALU.mult).then_inc(sq_made, 1)
                        lo_of(i * SLOTS + (first + SLOTS + j), j)
                        dve.wait_ge(ff_hi_made, i * SLOTS + (c * HALF_K + j + 1))
                        at = bass.ds(i * SLOTS + j, 1)
                        nc.vector.tensor_tensor(ff_lo[:, at].rearrange("p k s -> p (k s)"), sq_b[:, j % 2],
                                                ff_hi[:, at].rearrange("p k s -> p (k s)").bitcast(F32),
                                                ALU.subtract).then_inc(ff_lo_made, 1)
                if c == 0:
                    dve.wait_ge(ff_zeroed, 1)
                for h in range(2):
                    last_half = c == 1 and h == 1
                    for n in range(HALF_K // 2):
                        u = first + HALF_K + h * (HALF_K // 2) + n + SLOTS
                        if last_half and n == SLOTS:
                            break
                        if n == HALF_K // 2 - 1:
                            for t in range(TT):
                                dve.wait_ge(pe_done, BANK_DONE[u - SLOTS, t])
                                part = ff_sum[:, t, h * COL:(h + 1) * COL]
                                nc.vector.tensor_tensor(part, acc[:, t], part, ALU.add).then_inc(acc_to_dve, 1)
                        lo_of(u, n % SLOTS)
            dve.wait_ge(g_ff_in, 16)
            for t in range(TT):
                dve.wait_ge(ssq_act, Q_MIX + 2 * TT + t + 1)
                last = nc.vector.tensor_tensor(ff_sum[:, t, 0:COL], ff_sum[:, t, 0:COL], g_ff_post[:, 0:COL], ALU.mult)
            last.then_inc(half_scaled, 1)
            for t in range(TT):
                part = ff_sum[:, t, COL:D]
                dve.wait_ge(pe_done, BANK_DONE[UNITS - 1, t])
                nc.vector.tensor_tensor(part, acc[:, t], part, ALU.add).then_inc(acc_to_dve, 1)
                dve.wait_ge(acc_to_dve, V_FF + 3 * TT + t + 1)
                if t == 2:
                    dve.wait_ge(y_made, 2)
                if t == 3:
                    dve.wait_ge(y_made, 4)
                after(nc.vector.tensor_tensor(relu_b[:, t % 2], part, g_ff_post[:, COL:D], ALU.mult))
                dve.wait_ge(rstd_ff, t + 1)
                if t == 0:
                    dve.wait_ge(half_scaled, 2)
                for h, src in ((0, ff_sum[:, t, 0:COL]), (1, relu_b[:, t % 2])):
                    cols = slice(h * COL, (h + 1) * COL)
                    nc.vector.scalar_tensor_tensor(ff_sum[:, t, cols], src, rstd[:, 4, t:t + 1], x1[:, t, cols],
                                                   ALU.mult, ALU.add).then_inc(y_made, 1)

        @block.tensor
        def _(pe):
            def product(o, a, b, first, last):
                (a_hi, a_lo), (b_hi, b_lo) = a, b
                nc.tensor.matmul(o, a_hi, b_hi, start=first, stop=False)
                nc.tensor.matmul(o, a_hi, b_lo, start=False, stop=False)
                return nc.tensor.matmul(o, a_lo, b_hi, start=False, stop=last)

            def columns_unit(j, acts, bank, ks=range(KT)):
                hi, lo = stationary(w_hi, j), stationary(w_lo, j)
                for k in ks:
                    m = product(acc[:, bank], (hi[:, k], lo[:, k]), (acts[0][:, k], acts[1][:, k]),
                                k == 0, k == KT - 1)
                return m

            def rows_step(j, acts, k0, t, first, last):
                hi, lo = moving(w_hi, j), moving(w_lo, j)
                for q in range(2):
                    at = (slice(None), k0 + q, slice(t * P, (t + 1) * P))
                    m = product(acc[:, t], (acts[0][at], acts[1][at]), (hi[:, q], lo[:, q]),
                                first and q == 0, last and q == 1)
                return m

            def rows_block(acts, first_unit, units=SLOTS, bank_free=None, acts_ready=None):
                for n in range(units):
                    pe.wait_ge(lo_made, first_unit + (n + 1))
                    if acts_ready:
                        acts_ready(n)
                    for t in range(TT):
                        if n == 0 and bank_free:
                            bank_free(t)
                        m = rows_step(n % SLOTS, acts, 2 * n, t, n == 0, n == units - 1)
                        if n == units - 1 or t == TT - 1:
                            m.then_inc(pe_done, 1)

            actA, actB = (actA_hi, actA_lo), (actB_hi, actB_lo)

            def turn_tile(base, tile, t):
                pe.wait_ge(normed, (TT if base else 0) + t + 1)
                if t >= 2:
                    pe.wait_ge(turned_lo, base + t - 1)
                for k in range(KT):
                    m = nc.tensor.transpose(aux[:, 2 * (t % 2) + k // 4, (k % 4) * P:(k % 4 + 1) * P],
                                            tile[:, t, k * P:(k + 1) * P], ident[:])
                m.then_inc(turned, 1)

            pe.wait_ge(pool_consts, 1)
            for _ in range(WARM_UP):
                nc.tensor.transpose(acc[:, 3, 0:P], ident[:], ident[:])
            turn_tile(0, x0, 0)
            turn_tile(0, x0, 1)
            for n, t in ((0, 0), (0, 1), (1, 0), (1, 1), (0, 2), (1, 2), (0, 3), (1, 3)):
                pe.wait_ge(turned_lo, t + 1)
                pe.wait_ge(lo_made, n + 1)
                m = rows_step(n, actB, 2 * n, t, n == 0, False)
                if t == TT - 1:
                    m.then_inc(pe_done, 1)
                if n == 1 and t < 2:
                    turn_tile(0, x0, t + 2)
            for n in (2, 3):
                pe.wait_ge(lo_made, n + 1)
                for t in range(TT):
                    m = rows_step(n, actB, 2 * n, t, False, n == 3)
                    if n == 3 or t == TT - 1:
                        m.then_inc(pe_done, 1)
            with pe.Fori(1, 3) as b:
                rows_block(actB, b * SLOTS, bank_free=lambda t: pe.wait_ge(acc_to_act, b * TT + (t + 1 - TT)))

            def side_k(n, k):
                if k == 0:
                    pe.wait_ge(lo_made, U_SIDE + n + 1)
                    if n < 2:
                        pe.wait_ge(acc_to_dve, V_KV + n + 1)
                    else:
                        pe.wait_ge(acc_to_act, A_SIDE + n - 1)
                m = columns_unit(n % SLOTS, actB, n % 2, [k])
                if k == KT - 1:
                    m.then_inc(pe_done, 1)

            for n in range(SIDE_AHEAD):
                for k in range(KT):
                    side_k(n, k)
                for k in range(3 * n, 3 * n + 3):
                    if k == 0:
                        pe.wait_ge(rotated, 1)
                    if k == KT:
                        pe.wait_ge(rotated, 2)
                    if k >= 4:
                        pe.wait_ge(turned_lo, T_QK + k - 3)
                    for t in range(TT):
                        m = nc.tensor.transpose(aux[:, k % 4, t * P:(t + 1) * P],
                                                qk[:, t, 2 * k:2 * k + 2].rearrange("p h d -> p (h d)"), ident[:])
                    m.then_inc(turned, 1)

            def scores(s):
                b, g = divmod(s, NKV)
                if s == 0:
                    pe.wait_ge(turned_lo, T_FF)
                else:
                    pe.wait_ge(s_masked, s)
                k0 = max(b - 1, 0)
                for m2 in range(2):
                    for f in range(2):
                        q = q_pair[f][:, 2 * g + m2, P * b:P * b + P]
                        keys = (slice(None), g, slice(P * k0, P * b + P))
                        o = aux[:, f, 2 * P * (m2 + 1) - P * (b + 1 - k0):2 * P * (m2 + 1)]
                        nc.tensor.matmul(o, q, kT_hi[keys], start=True, stop=False)
                        m = nc.tensor.matmul(o, q, kT_lo[keys], start=False, stop=True)
                m.then_inc(s_done, 1)

            def turn_probs(s):
                pe.wait_ge(p_normed, s + 1)
                if s >= 2:
                    pe.wait_ge(pT_lo_made, s - 1)
                for h in range(QPK):
                    m = nc.tensor.transpose(aux[:, 2 + s % 2, P * h:P * h + P], probs[:, h, P:2 * P], ident[:])
                m.then_inc(pT_done, 1)

            def values(s):
                b, g = divmod(s, NKV)
                if b:
                    pe.wait_ge(pT_masked, 2 * (s - NKV) + 1)
                else:
                    pe.wait_ge(pT_lo_made, s + 1)
                if s < 2:
                    pe.wait_ge(acc_to_dve, V_KV + 3 + s)
                else:
                    pe.wait_ge(o_sum_made, s - 1)
                for kb in range(0 if b else 1, 2):
                    o, v = acc[:, 2 + s % 2], v_pair[:, b - 1 + kb, g]
                    nc.tensor.matmul(o, v, pT_hi[:, kb], start=kb == 0 or b == 0, stop=False)
                    if b and kb == 1:
                        pe.wait_ge(pT_masked, 2 * (s - NKV) + 2)
                    m = nc.tensor.matmul(o, v, pT_lo[:, kb], start=False, stop=kb == 1)
                m.then_inc(o_done, 1)

            done = 0
            for slot in range(SLOT_COUNT):
                while done < k_steps_until(slot):
                    side_k(SIDE_AHEAD + done // KT, done % KT)
                    done += 1
                if slot >= 2:
                    values(slot - 2)
                if slot < STEPS:
                    scores(slot)
                if 1 <= slot <= STEPS:
                    turn_probs(slot - 1)

            def vsgu_banks(t):
                if t < 2:
                    pe.wait_ge(acc_to_act, A_VSGU - 1 + t)
                else:
                    pe.wait_ge(o_sum_made, STEPS - 3 + t)

            rows_block(actB, U_VSGU, bank_free=vsgu_banks)
            pe.wait_ge(ws_in, 16)
            pe.wait_ge(s_masked, STEPS)
            for g in range(GROUPS):
                m = nc.tensor.transpose(aux[:, g // 4, (g % 4) * P:(g % 4 + 1) * P], w_s[:, g], ident[:])
                if g % 4 == 3:
                    m.then_inc(ws_turned, 1)
            rows_block(actB, U_VSGU + SLOTS, bank_free=lambda t: pe.wait_ge(acc_to_act, A_VSGU + t + 1))
            pe.wait_ge(o_lo_made, STEPS)
            for n in range(KT):
                pe.wait_ge(lo_made, U_WB + n + 1)
                if n < SLOTS:
                    pe.wait_ge(acc_to_act, A_VSGU + TT + n + 1)
                else:
                    pe.wait_ge(acc_to_dve, V_WB - SLOTS + n + 1)
                columns_unit(n % SLOTS, actA, n % 4).then_inc(pe_done, 1)
                for g in mix_groups_after(n):
                    if g == 0:
                        pe.wait_ge(w_mix_made, 1)
                        pe.wait_ge(v_normed, TT)
                    if g >= 4:
                        pe.wait_ge(a_made, g - 3)
                    for c in range(TT):
                        m = nc.tensor.matmul(aux[:, g % 4, c * P:(c + 1) * P], v_sgu[:, c, g * P:(g + 1) * P],
                                             w_mix[:, g], start=True, stop=True)
                    m.then_inc(mix_done, 1)
            with pe.Fori(0, 2) as i:
                for j in range(SLOTS):
                    pe.wait_ge(lo_made, i * SLOTS + (U_WA + j + 1))
                    pe.wait_ge(acc_to_dve, i * SLOTS + (V_WA - SLOTS + j + 1))
                    for k in range(KT):
                        pe.wait_ge(a_lo, k + 1)
                        m = columns_unit(j, actB, j, [k])
                    m.then_inc(pe_done, 1)
            rows_block(actA, U_WO, bank_free=lambda t: pe.wait_ge(acc_to_dve, V_WO - TT + t + 1),
                       acts_ready=lambda n: pe.wait_ge(merged_lo, 2 * n + 2))

            def half_unit(j, tokens):
                for k in range(KT):
                    hi, lo = stationary(w_hi, j)[:, k], stationary(w_lo, j)[:, k]
                    m = product(acc[:, j, tokens], (hi, lo), (actB_hi[:, k, tokens], actB_lo[:, k, tokens]),
                                k == 0, k == KT - 1)
                return m

            for t in range(TT):
                pe.wait_ge(acc_to_act, A_WO + t + 1)
                for n in range(SLOTS):
                    if t == 0:
                        pe.wait_ge(lo_made, U_WO + SLOTS + n + 1)
                    m = rows_step(n, actA, 2 * n, t, n == 0, n == SLOTS - 1)
                    if t == TT - 1 or n == SLOTS - 1:
                        m.then_inc(pe_done, 1)
                    if t >= 2 and n == 3 - t:
                        turn_tile(T_FF, mix, t - 2)
            for j in range(SLOTS):
                pe.wait_ge(lo_made, U_FF + j + 1)
                pe.wait_ge(acc_to_dve, V_WO + j + 1)
                pe.wait_ge(turned_lo, T_FF + 2)
                half_unit(j, slice(0, 2 * P))
                if j in (1, 2):
                    turn_tile(T_FF, mix, j + 1)
            for j in range(SLOTS):
                pe.wait_ge(turned_lo, T_FF + TT)
                half_unit(j, slice(2 * P, S)).then_inc(pe_done, 1)
            for c in range(2):
                first = U_FF + c * U_HALF
                relus = A_FF + c * HALF_K
                with pe.Fori(0 if c else 1, HALF_K // SLOTS) as i:
                    for j in range(SLOTS):
                        pe.wait_ge(lo_made, i * SLOTS + (first + j + 1))
                        pe.wait_ge(acc_to_act, i * SLOTS + (relus - SLOTS + j + 1))
                        if c == 1:
                            pe.wait_ge(acc_to_dve, V_FF + TT + j + 1)
                        m = columns_unit(j, actB, j)
                        m.then_inc(pe_done, 1)
                ff = (ff_hi, ff_lo)
                rows_block(ff, first + HALF_K, units=HALF_K // 2,
                           bank_free=lambda t: pe.wait_ge(acc_to_act, relus + HALF_K - SLOTS + t + 1),
                           acts_ready=lambda n: pe.wait_ge(ff_lo_made, c * HALF_K + 2 * n + 2))
                if c == 0:
                    rows_block(ff, first + HALF_K + HALF_K // 2, units=HALF_K // 2,
                               bank_free=lambda t: pe.wait_ge(acc_to_dve, V_FF + t + 1))
                else:
                    last = first + HALF_K + HALF_K // 2
                    for n in range(SLOTS):
                        pe.wait_ge(lo_made, last + n + 1)
                        for t in range(TT):
                            if n == 0:
                                pe.wait_ge(acc_to_dve, V_FF + 2 * TT + t + 1)
                            m = rows_step(n, ff, 2 * n, t, n == 0, False)
                        m.then_inc(pe_done, 1)
                    for t in range(TT):
                        for n in range(SLOTS, HALF_K // 2):
                            if t == 0:
                                pe.wait_ge(lo_made, last + n + 1)
                            m = rows_step(n % SLOTS, ff, 2 * n, t, False, n == HALF_K // 2 - 1)
                            if t == TT - 1 or n == HALF_K // 2 - 1:
                                m.then_inc(pe_done, 1)


INPUTS = ["x", "positions", "w_in", "ln_v_gain", "ln_v_bias", "w_spatial", "b_spatial", "sinks", "w_a", "w_b",
          "w_o", "norm_mix_pre", "norm_mix_post", "w_ff_in", "w_ff_out", "norm_ff_pre", "norm_ff_post"]


def kernel(**inputs):
    import concourse.bacc as bacc
    from concourse.bass_utils import run_bass_kernel_spmd

    nc = bacc.Bacc("TRN2", target_bir_lowering=False, num_devices=1)
    arrays, args = {}, []
    for name in INPUTS:
        a = np.ascontiguousarray(inputs[name])
        arrays[f"in_{name}"] = a
        args.append(nc.dram_tensor(f"in_{name}", a.shape, mybir.dt.from_np(a.dtype), kind="ExternalInput").ap())
    result = nc.dram_tensor("out", (1, S, D), F32, kind="ExternalOutput").ap()
    hybrid_block(nc, *args, result)
    r = run_bass_kernel_spmd(nc, [arrays], core_ids=[0])
    return r.results[0]["out"]
```
